# Optimizing a Trainium2 kernel written in Bass

```python
import math
import jax, jax.numpy as jnp
from jax import lax
import numpy as np

D_MODEL = 1024
BATCH = 1
SEQ = 256
DEPTH = 2

N_EVEN = (DEPTH + 1) // 2
N_ODD = DEPTH // 2
RMS_EPS = 1e-6
SSM_GROUP = 16
SSM_GROUPS = D_MODEL // SSM_GROUP
SSM_STATE = 64
SSM_CHUNK = 128
DT_MIN = 1e-3
DT_MAX = 1e-1
MLA_HEADS = 16
MLA_NOPE = 64
MLA_ROPE = 32
MLA_V = 64
MLA_QK = MLA_NOPE + MLA_ROPE
MLA_Q_RANK = 384
MLA_KV_RANK = 256
ROPE_THETA = 10000.0
Q_BLOCK = 128
FFN_DIM = 2816
N_EXPERTS = 8
TOP_K = 2
EXPERT_DIM = 1792

kernel_name = 'hybrid_s5_mla_moe_sandwich_adaln'

def rms_norm(x, g):
    xf = x.astype(jnp.float32)
    y = xf * lax.rsqrt(jnp.mean(xf * xf, axis=-1, keepdims=True) + RMS_EPS)
    return (y * g.astype(jnp.float32)).astype(x.dtype)

def modulate(h, shift, scale):
    return h * (1 + scale[:, None, :]) + shift[:, None, :]

def cmul(ar, ai, br, bi):
    return ar * br - ai * bi, ar * bi + ai * br

def s5_mixer(u, a_re, a_im, log_dt, b_re, b_im, c_re, c_im, d, w_glu):
    bsz, seq, _ = u.shape
    f32 = jnp.float32
    a_re = a_re.astype(f32)
    a_im = a_im.astype(f32)
    dt = jnp.exp(log_dt.astype(f32))[:, None]
    mag = jnp.exp(a_re * dt)
    ab_re, ab_im = mag * jnp.cos(a_im * dt), mag * jnp.sin(a_im * dt)
    den = a_re * a_re + a_im * a_im
    num_re, num_im = ab_re - 1.0, ab_im
    f_re = (num_re * a_re + num_im * a_im) / den
    f_im = (num_im * a_re - num_re * a_im) / den
    bb_re, bb_im = cmul(f_re[..., None], f_im[..., None], b_re.astype(f32), b_im.astype(f32))
    c_re = c_re.astype(f32)
    c_im = c_im.astype(f32)
    n_chunks = seq // SSM_CHUNK
    uf = u.astype(f32)
    u_chunks = uf.reshape(bsz, n_chunks, SSM_CHUNK, SSM_GROUPS, SSM_GROUP).transpose(1, 2, 0, 3, 4)
    a_el_re = jnp.broadcast_to(ab_re, (SSM_CHUNK, 1, SSM_GROUPS, SSM_STATE))
    a_el_im = jnp.broadcast_to(ab_im, (SSM_CHUNK, 1, SSM_GROUPS, SSM_STATE))

    def combine(e1, e2):
        a1r, a1i, b1r, b1i = e1
        a2r, a2i, b2r, b2i = e2
        ar, ai = cmul(a2r, a2i, a1r, a1i)
        br, bi = cmul(a2r, a2i, b1r, b1i)
        return ar, ai, br + b2r, bi + b2i

    def chunk_step(carry, u_c):
        h0r, h0i = carry
        bu_re = jnp.einsum('tbgh,gph->tbgp', u_c, bb_re)
        bu_im = jnp.einsum('tbgh,gph->tbgp', u_c, bb_im)
        acr, aci, hr, hi = lax.associative_scan(combine, (a_el_re, a_el_im, bu_re, bu_im), axis=0)
        pr, pi = cmul(acr, aci, h0r[None], h0i[None])
        hr = hr + pr
        hi = hi + pi
        y = jnp.einsum('tbgp,ghp->tbgh', hr, c_re) - jnp.einsum('tbgp,ghp->tbgh', hi, c_im)
        return (hr[-1], hi[-1]), y

    h_init = (jnp.zeros((bsz, SSM_GROUPS, SSM_STATE), f32), jnp.zeros((bsz, SSM_GROUPS, SSM_STATE), f32))
    _, ys = lax.scan(chunk_step, h_init, u_chunks)
    y = ys.transpose(2, 0, 1, 3, 4).reshape(bsz, seq, D_MODEL)
    y = (y + d.astype(f32) * uf).astype(u.dtype)
    z = jax.nn.gelu(y)
    gl = z @ w_glu
    return gl[..., :D_MODEL] * jax.nn.sigmoid(gl[..., D_MODEL:])

def rope(x, cos, sin):
    half = MLA_ROPE // 2
    xf = x.astype(jnp.float32)
    x1, x2 = xf[..., :half], xf[..., half:]
    return jnp.concatenate([x1 * cos - x2 * sin, x1 * sin + x2 * cos], axis=-1).astype(x.dtype)

def mla_mixer(h, positions, w_in, q_norm, kv_norm, w_uq, w_ukv, w_o):
    bsz, seq, _ = h.shape
    proj = h @ w_in
    cq = rms_norm(proj[..., :MLA_Q_RANK], q_norm)
    ckv = rms_norm(proj[..., MLA_Q_RANK:MLA_Q_RANK + MLA_KV_RANK], kv_norm)
    k_rope_in = proj[..., MLA_Q_RANK + MLA_KV_RANK:]
    q = (cq @ w_uq).reshape(bsz, seq, MLA_HEADS, MLA_QK)
    kv = (ckv @ w_ukv).reshape(bsz, seq, MLA_HEADS, MLA_NOPE + MLA_V)
    k_nope, v = kv[..., :MLA_NOPE], kv[..., MLA_NOPE:]
    half = MLA_ROPE // 2
    inv_freq = ROPE_THETA ** (-jnp.arange(half, dtype=jnp.float32) / half)
    ang = positions.astype(jnp.float32)[..., None, None] * inv_freq
    cos, sin = jnp.cos(ang), jnp.sin(ang)
    q = jnp.concatenate([q[..., :MLA_NOPE], rope(q[..., MLA_NOPE:], cos, sin)], axis=-1)
    k_rope = rope(k_rope_in[:, :, None, :], cos, sin)
    k = jnp.concatenate([k_nope, jnp.broadcast_to(k_rope, (bsz, seq, MLA_HEADS, MLA_ROPE))], axis=-1)
    n_blocks = seq // Q_BLOCK
    q_blocks = q.reshape(bsz, n_blocks, Q_BLOCK, MLA_HEADS, MLA_QK).transpose(1, 0, 2, 3, 4)
    key_idx = jnp.arange(seq)
    sm_scale = MLA_QK ** -0.5

    def attend(args):
        q_blk, blk = args
        q_idx = blk * Q_BLOCK + jnp.arange(Q_BLOCK)
        s = jnp.einsum('bqhd,bkhd->bhqk', q_blk, k, preferred_element_type=jnp.float32) * sm_scale
        s = jnp.where(key_idx[None, :] <= q_idx[:, None], s, -jnp.inf)
        p = jax.nn.softmax(s, axis=-1).astype(v.dtype)
        return jnp.einsum('bhqk,bkhd->bqhd', p, v)

    o = lax.map(attend, (q_blocks, jnp.arange(n_blocks)))
    o = o.transpose(1, 0, 2, 3, 4).reshape(bsz, seq, MLA_HEADS * MLA_V)
    return o @ w_o

def dense_swiglu(h, w_in, w_out):
    gu = h @ w_in
    return (jax.nn.silu(gu[..., :FFN_DIM]) * gu[..., FFN_DIM:]) @ w_out

def moe_swiglu(h, w_router, b_router, w_in, w_out):
    bsz, seq, d = h.shape
    t = h.reshape(-1, d)
    logits = (t @ w_router).astype(jnp.float32) + b_router.astype(jnp.float32)
    top_val, top_idx = lax.top_k(logits, TOP_K)
    top_w = jax.nn.softmax(top_val, axis=-1)
    comb = jnp.sum(jax.nn.one_hot(top_idx, N_EXPERTS, dtype=jnp.float32) * top_w[..., None], axis=1)
    out = jnp.zeros_like(t)
    for e in range(N_EXPERTS):
        gu = t @ w_in[e]
        y_e = (jax.nn.silu(gu[:, :EXPERT_DIM]) * gu[:, EXPERT_DIM:]) @ w_out[e]
        out = out + comb[:, e:e + 1].astype(t.dtype) * y_e
    return out.reshape(bsz, seq, d)

def setup_inputs(seed: int = 0) -> dict:
    key = jax.random.key(seed)
    ks = iter(jax.random.split(key, 32))
    f32 = jnp.float32

    def nrm(shape, scale):
        return jax.random.normal(next(ks), shape, f32) * scale

    x = nrm((BATCH, SEQ, D_MODEL), 1.0)
    c = nrm((BATCH, D_MODEL), 1.0)
    offset = jax.random.randint(next(ks), (BATCH, 1), 0, 4096, dtype=jnp.int32)
    positions = offset + jnp.arange(SEQ, dtype=jnp.int32)[None, :]
    norm_g = 1.0 + nrm((DEPTH, 4, D_MODEL), 0.01)
    w_ada = nrm((DEPTH, D_MODEL, 6 * D_MODEL), 0.5 * D_MODEL ** -0.5)
    b_ada = nrm((DEPTH, 6 * D_MODEL), 0.02)
    n_idx = jnp.arange(SSM_STATE, dtype=f32)
    ssm_a_re = -0.5 + nrm((N_EVEN, SSM_GROUPS, SSM_STATE), 0.01)
    ssm_a_im = math.pi * n_idx + nrm((N_EVEN, SSM_GROUPS, SSM_STATE), 0.01)
    ssm_log_dt = jax.random.uniform(next(ks), (N_EVEN, SSM_GROUPS), f32, math.log(DT_MIN), math.log(DT_MAX))
    ssm_b_re = nrm((N_EVEN, SSM_GROUPS, SSM_STATE, SSM_GROUP), (2 * SSM_GROUP) ** -0.5)
    ssm_b_im = nrm((N_EVEN, SSM_GROUPS, SSM_STATE, SSM_GROUP), (2 * SSM_GROUP) ** -0.5)
    ssm_c_re = nrm((N_EVEN, SSM_GROUPS, SSM_GROUP, SSM_STATE), (2 * SSM_STATE) ** -0.5)
    ssm_c_im = nrm((N_EVEN, SSM_GROUPS, SSM_GROUP, SSM_STATE), (2 * SSM_STATE) ** -0.5)
    ssm_d = nrm((N_EVEN, D_MODEL), 1.0)
    ssm_w_glu = nrm((N_EVEN, D_MODEL, 2 * D_MODEL), D_MODEL ** -0.5)
    ffn_w_in = nrm((N_EVEN, D_MODEL, 2 * FFN_DIM), D_MODEL ** -0.5)
    ffn_w_out = nrm((N_EVEN, FFN_DIM, D_MODEL), FFN_DIM ** -0.5)
    mla_w_in = nrm((N_ODD, D_MODEL, MLA_Q_RANK + MLA_KV_RANK + MLA_ROPE), D_MODEL ** -0.5)
    mla_q_norm = 1.0 + nrm((N_ODD, MLA_Q_RANK), 0.01)
    mla_kv_norm = 1.0 + nrm((N_ODD, MLA_KV_RANK), 0.01)
    mla_w_uq = nrm((N_ODD, MLA_Q_RANK, MLA_HEADS * MLA_QK), MLA_Q_RANK ** -0.5)
    mla_w_ukv = nrm((N_ODD, MLA_KV_RANK, MLA_HEADS * (MLA_NOPE + MLA_V)), MLA_KV_RANK ** -0.5)
    mla_w_o = nrm((N_ODD, MLA_HEADS * MLA_V, D_MODEL), (MLA_HEADS * MLA_V) ** -0.5)
    moe_w_router = nrm((N_ODD, D_MODEL, N_EXPERTS), D_MODEL ** -0.5)
    moe_b_router = nrm((N_ODD, N_EXPERTS), 0.01)
    moe_w_in = nrm((N_ODD, N_EXPERTS, D_MODEL, 2 * EXPERT_DIM), D_MODEL ** -0.5)
    moe_w_out = nrm((N_ODD, N_EXPERTS, EXPERT_DIM, D_MODEL), EXPERT_DIM ** -0.5)
    return {'x': x, 'c': c, 'positions': positions, 'norm_g': norm_g, 'w_ada': w_ada, 'b_ada': b_ada,
            'ssm_a_re': ssm_a_re, 'ssm_a_im': ssm_a_im, 'ssm_log_dt': ssm_log_dt,
            'ssm_b_re': ssm_b_re, 'ssm_b_im': ssm_b_im, 'ssm_c_re': ssm_c_re, 'ssm_c_im': ssm_c_im,
            'ssm_d': ssm_d, 'ssm_w_glu': ssm_w_glu, 'ffn_w_in': ffn_w_in, 'ffn_w_out': ffn_w_out,
            'mla_w_in': mla_w_in, 'mla_q_norm': mla_q_norm, 'mla_kv_norm': mla_kv_norm,
            'mla_w_uq': mla_w_uq, 'mla_w_ukv': mla_w_ukv, 'mla_w_o': mla_w_o,
            'moe_w_router': moe_w_router, 'moe_b_router': moe_b_router,
            'moe_w_in': moe_w_in, 'moe_w_out': moe_w_out}

def reference(x, c, positions, norm_g, w_ada, b_ada,
              ssm_a_re, ssm_a_im, ssm_log_dt, ssm_b_re, ssm_b_im, ssm_c_re, ssm_c_im,
              ssm_d, ssm_w_glu, ffn_w_in, ffn_w_out,
              mla_w_in, mla_q_norm, mla_kv_norm, mla_w_uq, mla_w_ukv, mla_w_o,
              moe_w_router, moe_b_router, moe_w_in, moe_w_out):
    c_act = jax.nn.silu(c)
    for i in range(DEPTH):
        j = i // 2
        mod = c_act @ w_ada[i] + b_ada[i]
        sh1, sc1, g1 = mod[:, :D_MODEL], mod[:, D_MODEL:2 * D_MODEL], mod[:, 2 * D_MODEL:3 * D_MODEL]
        sh2, sc2, g2 = mod[:, 3 * D_MODEL:4 * D_MODEL], mod[:, 4 * D_MODEL:5 * D_MODEL], mod[:, 5 * D_MODEL:]
        h = modulate(rms_norm(x, norm_g[i, 0]), sh1, sc1)
        if i % 2 == 0:
            h = s5_mixer(h, ssm_a_re[j], ssm_a_im[j], ssm_log_dt[j], ssm_b_re[j], ssm_b_im[j],
                         ssm_c_re[j], ssm_c_im[j], ssm_d[j], ssm_w_glu[j])
        else:
            h = mla_mixer(h, positions, mla_w_in[j], mla_q_norm[j], mla_kv_norm[j],
                          mla_w_uq[j], mla_w_ukv[j], mla_w_o[j])
        x = x + g1[:, None, :] * rms_norm(h, norm_g[i, 1])
        h = modulate(rms_norm(x, norm_g[i, 2]), sh2, sc2)
        if i % 2 == 0:
            h = dense_swiglu(h, ffn_w_in[j], ffn_w_out[j])
        else:
            h = moe_swiglu(h, moe_w_router[j], moe_b_router[j], moe_w_in[j], moe_w_out[j])
        x = x + g2[:, None, :] * rms_norm(h, norm_g[i, 3])
    return x


_drawn_inputs = setup_inputs


def setup_inputs(seed=0):
    import zlib

    import numpy as np

    out = dict(_drawn_inputs(seed))
    spreads = {}
    factors = {'norm_g': 3.461,
     'ssm_a_re': 8.0,
     'ssm_b_re': 2.941,
     'ssm_b_im': 3.047,
     'ssm_c_re': 4.09,
     'ssm_c_im': 3.07,
     'mla_q_norm': 8.0,
     'mla_kv_norm': 8.0,
     'moe_b_router': 12.352}
    for name, (base, spread) in spreads.items():
        noise = np.random.default_rng([zlib.crc32(name.encode()), seed]).standard_normal(out[name].shape)
        drawn = base * np.exp(spread * noise) if base else spread * noise
        out[name] = __import__('jax').numpy.asarray(drawn.astype(out[name].dtype))
    for name, factor in factors.items():
        out[name] = (out[name] * factor).astype(out[name].dtype)
    return out
```

```python
import math
from contextlib import ExitStack

import numpy as np
import concourse.bass as bass
from concourse import mybir

F32, F32R, I32, U32 = mybir.dt.float32, mybir.dt.float32r, mybir.dt.int32, mybir.dt.uint32
ALU, ACT, AX = mybir.AluOpType, mybir.ActivationFunctionType, mybir.AxisListType

P = 128
D = 1024
DT = D // P
SEQ = 256
TT = SEQ // P
EPS = 1e-6
NG, GH, NS, L = 64, 16, 64, 8
NJ = SEQ // L
GI = NG // 2
O_ON_POOL = 6
FFN, NE, ED, FB = 2816, 8, 1792, 256
FSTEPS, MSTEPS = FFN // FB, ED // FB
H, NOPE, ROPE, VD = 16, 64, 32, 64
QK = NOPE + ROPE
QR, KR = 384, 256
PROJ = QR + KR + ROPE
HALF = ROPE // 2
SCALE = QK ** -0.5
NEG = -1e30
RING = 6
UNIT = 2048
NSEC = 12
GATES = (2, 5, 8, 11)
TWO_PI_1 = 6.28125
TWO_PI_2 = float(np.float32(round((2 * math.pi - TWO_PI_1) * 2 ** 21) / 2 ** 21))
TWO_PI_3 = float(np.float32(2 * math.pi - TWO_PI_1 - TWO_PI_2))
INV_2PI = float(np.float32(1 / (2 * math.pi)))
ROUND = float(1.5 * 2 ** 23)
PI_SAFE = 3.1415925


def ADA_PER_STEP(t):
    return 2 if t else 4


def raw_stream():
    s = [("ada", n) for n in range(24)]
    w = iter(range(10 ** 6))
    s += [("w", next(w)) for _ in range(8)]
    ada = list(range(24, 48))
    for step in range(FSTEPS + 1):
        for _ in range(2 if step == 0 else 1 if step == FSTEPS else 3):
            s.append(("w", next(w)))
        if step < FSTEPS:
            for _ in range(ADA_PER_STEP(step)):
                s.append(("ada", ada.pop(0)))
    assert not ada
    n_rest = 12 + NE * MSTEPS * 3
    s += [("w", next(w)) for _ in range(n_rest)]
    return s


STREAM = raw_stream()
V_GLU = 0
V_FFN = 8
V_MLA = V_FFN + 3 * FSTEPS
V_MOE = V_MLA + 12
V_ALL = V_MOE + 3 * MSTEPS * NE
RAW_OF_ADA = {n: r for r, (k, n) in enumerate(STREAM) if k == "ada"}
RAW_OF_W = {n: r for r, (k, n) in enumerate(STREAM) if k == "w"}


def loads_of(kind, n):
    if kind == "ada" or V_MLA <= n < V_MOE:
        return 1
    if n < V_FFN:
        return 2
    m, steps = (n - V_FFN, FSTEPS) if n < V_MLA else (n - V_MOE, MSTEPS * NE)
    return 1 if m == 3 * steps - 1 or (m >= 2 and (m + 1) % 3 == 2) else 2


RAW_COUNT, _slots = [], [0] * RING
for _r, (_k, _n) in enumerate(STREAM):
    _slots[_r % RING] += 16 * loads_of(_k, _n)
    RAW_COUNT.append(_slots[_r % RING])


def program(nc, x_in, c_in, pos_in, norm_g, w_ada, b_ada, a_re, a_im, log_dt, b_re, b_im, c_re, c_im, d_in,
            w_glu, ffn_in, ffn_out, mla_in, q_norm, kv_norm, w_uq, w_ukv, w_o, w_router, b_router,
            moe_in, moe_out, out):
    ctx = ExitStack()
    with ctx:
        KB = 1024
        BASE = 16512
        def at(name, shape, kb, dtype=F32):
            return nc.alloc_sbuf_tensor_at(name, shape, dtype, offset=BASE + int(kb * KB))

        def sem(name):
            return ctx.enter_context(nc.semaphore(name))

        def scratch(name, shape):
            return nc.dram_tensor(name, shape, F32, kind="Internal").ap()

        RAW = at("raw", [P, RING, UNIT], 0)
        HI = at("w_hi", [P, RING, UNIT], 48, F32R)
        LO = at("w_lo", [P, RING, UNIT], 96, F32R)
        O = at("s5_out_map", [P, 2, GI, L + 1, GH], 48)
        RT = at("s5_in_map", [P, 2, GI, P], 84)
        M = at("s5_chunk_map", [P, NG, P], 116)
        TAB = at("s5_phase", [P, 2, GI, NJ], 148)
        G = at("s5_g", [P, 2, GI, NJ], 156)
        XN0 = at("xn0", [P, TT, D], 156)
        TMP = at("s5_tmp", [P, 2, GI, NJ], 164)
        RTMP = at("s5_rtmp", [P, 2, 512], 164)
        R8T = at("s5_r8", [P, GI, NJ], 168)
        OTMP = at("s5_otmp", [P, 2, 512], 168)
        S = at("s5_state", [P, 2, GI, NJ], 172)
        STRIP = at("s5_strip", [P, 16, P], 172)
        U = at("s5_u", [P, NG, NJ], 180)
        RBLK = at("s5_rblk", [P, 2, 4, L, GH], 180)
        BB = at("s5_bb", [P, 2, GI, GH], 184)
        UT = at("u_t", [P, DT, L, NJ], 188)
        Y1 = at("s5_y1", [P, 16, P], 164)
        Y2 = at("s5_y2", [P, 16, 4, NJ], 156)
        YT = at("y_t", [P, DT, L, NJ], 152)
        BN = at("b_nat", [P, 2, GI, GH], 116)
        CN = at("c_nat", [P, 2, 4, 2, NS], 120)
        CT = at("c_t", [P, 2, GI, GH], 124)
        PW = at("a_pow", [P, 4, GI, L + 1], 128)
        PWR = at("a_pow_rev", [P, 2, GI, L], 132.5)
        SM = at("s5_small", [P, 36, GI], 134.5)
        ROWS = at("param_rows", [96, P], 139)
        AROWS = at("a_rows", [96, 2, NS], 139.5)
        LDT = at("ldt_rows", [96, 2], 140)
        AT = at("a_t", [P, 96], 140.5)
        X = at("x", [P, TT, D], 144)
        TOK = at("tok", [P, TT, D], 152)
        AH = at("act_hi", [P, DT, SEQ], 160, F32R)
        AL = at("act_lo", [P, DT, SEQ], 168, F32R)
        H32 = at("act_f32", [P, DT, SEQ], 176)
        JUNK = at("junk", [P, 2, D], 176)
        JUNK0 = at("junk0", [P, 2, D], 188)
        RES = at("res_tmp", [P, 4, 512], 176)
        SG = at("glu_sig", [P, 2, TT, FB], 184)
        GTH = at("gt_hi", [P, 4, SEQ], 184, F32R)
        GTL = at("gt_lo", [P, 4, SEQ], 188, F32R)
        FS = at("ffn_silu", [P, 4, SEQ], 176)
        FP = at("ffn_prod", [P, 4, SEQ], 180)
        GROW = at("gate_row", [P, D], 192)
        WIDE = at("ada_wide", [P, 2, 256], 196)
        MROW = at("mod_rows", [4, 2, 256], 198)
        BROW = at("bias_rows", [4, 2, 256], 200)
        NROW = at("norm_rows", [4, 2, 256], 202)
        Q = at("q_tok", [P, TT, H, QK], 144)
        PR = at("mla_proj", [P, TT, PROJ], 152)
        CQH = at("cq_hi", [P, 5, SEQ], 160, F32R)
        CQL = at("cq_lo", [P, 5, SEQ], 165, F32R)
        KF = at("k_tok", [P, TT, H, QK], 176)
        VV = at("v_tok", [P, TT, H, VD], 188)
        OTH = at("o_hi", [P, DT, SEQ], 160, F32R)
        OTL = at("o_lo", [P, DT, SEQ], 168, F32R)
        QKT = at("qk_t", [QK, 2, 2, SEQ], 156)
        PB = at("probs", [P, 2, 384], 196)
        PTB = at("probs_t", [P, 2, 384], 199)
        RTM = at("rope_tmp", [P, 4, H, HALF], 199)
        C32 = at("cq_f32", [P, 5, SEQ], 176)
        ROT = at("rope_ang", [P, 8, TT, HALF], 196)
        XEH = at("xe_hi", [P, 2, DT, P], 160, F32R)
        XEL = at("xe_lo", [P, 2, DT, P], 168, F32R)
        ONE = at("one_hot", [P, 2, TT, P], 176)
        HOT = at("hot_cols", [P, 2, 2, TT], 178)
        YACC = at("y_acc", [P, TT, D], 184)
        YSB = at("y_e", [P, D], 192)
        XE32 = at("xe_f32", [P, DT, P], 192)
        EGH = at("e_hi", [P, 2, 2, P], 196, F32R)
        EGL = at("e_lo", [P, 2, 2, P], 198, F32R)
        ESI = at("e_silu", [P, 2, FB], 200)
        EPR = at("e_prod", [P, 2, FB], 202)
        TRI = at("tri", [P, P], 196)
        ONES = at("ones", [P, P], 196.5)
        WR = at("w_router_sb", [P, DT, NE], 197)
        LGT = at("lg_t", [NE, SEQ], 197.5)
        BRT = at("b_router_sb", [P, NE], 198.5)
        VG = at("v_gate_up", [P, 2, DT, 2, FB], 0)
        VDN = at("v_down", [P, 2, 2, D], 32)
        VX = at("v_x", [P, DT, P], 160)
        VY = at("v_y", [P, D], 164)
        VT = at("v_prod_t", [P, 2, 2, P], 168)
        VC = at("v_cols", [P, 2, TT], 170)
        VH = at("v_one_hot", [P, 2, TT, P], 176)
        kc = 204
        IDENT = at("ident", [P, P], kc)
        VEC = at("vec_t", [P, 88], kc + .5)
        MOD = at("mod_t", [P, NSEC, DT], kc + .875)
        CS = at("rope_cs", [P, 2, TT, HALF], kc + 1.25)
        ST = at("stats", [P, 32], kc + 1.5)
        CB = at("c_bcast", [P, DT, 32], kc + 1.625)
        MASK = at("mask", [P, SEQ], kc + 1.625)
        PT = at("one_hot_t", [P, SEQ], kc + 1.625)
        IOTA = at("iota", [P, P], kc + 2.625)
        IOTI = nc.alloc_sbuf_tensor_at("iota_i", [P, P], I32, offset=BASE + int(142 * KB))
        PS = ctx.enter_context(nc.psum_tensor("ps", [P, 8, 512], F32))
        LG = at("logits", [P, TT, NE], 200)
        M8 = at("top8", [P, TT, 8], 200.125)
        I8 = nc.alloc_sbuf_tensor_at("top8_idx", [P, TT, 8], U32, offset=BASE + int(200.25 * KB))
        IF = at("top_idx_f", [P, TT, 2], 200.375)
        WT = at("top_w", [P, 4, TT], 200.5)
        SEL = at("sel", [P, 2, TT, NE], 200.625)
        COMB = at("comb", [P, TT, NE], 200.875)
        MSK = at("chosen", [P, TT, NE], 201)
        SLOT = at("slot_of", [P, TT, NE], kc + 3.125)
        COMBP = at("comb_keep", [P, TT, NE], kc + 3.125 + 0.0625)
        POSI = nc.alloc_sbuf_tensor_at("pos_i", [P, TT], I32, offset=BASE + int((kc + 3.125 + 0.125) * KB))
        POSF = at("pos_f", [P, TT], kc + 3.125 + .15625)
        EPSC = at("eps_c", [P, 1], kc + 3.125 + .1875)
        WSL = at("slot_w", [P, 1], kc + 3.125 + .28125)
        CNT = nc.alloc_sbuf_tensor_at("expert_counts", [P, 16], I32, offset=BASE + int((kc + 3.125 + .3125) * KB))
        INVF = at("inv_freq", [P, HALF], kc + 3.125 + .21875)

        scr_u = scratch("scr_u", [D, L, NJ])
        scr_y = scratch("scr_y", [D, L, NJ])
        scr_gate = scratch("scr_gate", [4, D])
        scr_x = scratch("scr_x", [SEQ, D])

        raw_in = [sem(f"raw_in{i}") for i in range(RING)]
        row_in = [sem(f"row_in{i}") for i in range(2)]
        bias_in = [sem(f"bias_in{i}") for i in range(2)]
        gate_out = [sem(f"gate_out{i}") for i in range(4)]

        def sems(text):
            return [sem(n) for n in text.split()]

        ada_used, hi_done, lo_done, unit_used = sems("ada_used hi_done lo_done unit_used")
        at_ok, ident_ok, iota_ok, rows_in, a_in, bn_in, cn_in, x_ld, pos_ld = sems(
            "at_ok ident_ok iota_ok rows_in a_in bn_in cn_in x_ld pos_ld")
        vec_ps, vec_ok, ldt_ok, at_ps, ct_ps, ct_ok, cact_ok, cb_ok = sems(
            "vec_ps vec_ok ldt_ok at_ps ct_ps ct_ok cact_ok cb_ok")
        wide_ok, mrow_ok, mod_ps, mod_ok, gate_in, mask_ok = sems("wide_ok mrow_ok mod_ps mod_ok gate_in mask_ok")
        dch, ach, pch = sems("dve_chain act_chain pool_chain")
        dt_ok, tre_ok, ang_ok, fun_ok, pw_ok, bb_ok = sems("dt_ok tre_ok ang_ok fun_ok pw_ok bb_ok")
        rblk_ok, rt_ps, rt_ok, o_ok, strip_ps, strip_ok, m_zero, m_in, tab_ok = sems(
            "rblk_ok rt_ps rt_ok o_ok strip_ps strip_ok m_zero m_in tab_ok")
        n_ss, n_rt, n_tok, n_ps, n_f32, n_hi, n_lo = sems("n_ss n_rt n_tok n_ps n_f32 n_hi n_lo")
        u_out, u_in, v_ps, s_ok, y_ps, y1_ok, y2_ps, y2_ok, y_out, yt_in, yt_ok, zh_ok, zl_ok = sems(
            "u_out u_in v_ps s_ok y_ps y1_ok y2_ps y2_ok y_out yt_in yt_ok zh_ok zl_ok")
        glu_mm, sig_ok, glu_ok = sems("glu_mm sig_ok glu_ok")
        r_ss, r_sum, r_rt, res_ok = sems("r_ss r_sum r_rt res_ok")
        f_mm, f_silu, f_prod, f_hi, f_lo = sems("f_mm f_silu f_prod f_hi f_lo")
        x_out, p_sb, p_rt, p_nrm, p_ps, p_f32, p_hi, p_lo = sems(
            "x_out p_sb p_rt p_nrm p_ps p_f32 p_hi p_lo")
        cs_arg, cs_ok, q_sb, q_rope, k_rope, kf_ok, vv_ok = sems(
            "cs_arg cs_ok q_sb q_rope k_rope kf_ok vv_ok")
        qk_ps, qk_sb, s_mm, s_max, e_ok, pn_ok, pt_ps, pt_sb, o_mm, o_hi, o_lo = sems(
            "qk_ps qk_sb s_mm s_max e_ok pn_ok pt_ps pt_sb o_mm o_hi o_lo")
        rc_in, tri_ok, lgt_mm, lgt_sb, lg_ps, td_ok, te_ok, msk_ok, pos_ps, hot_ok, ovf_ok = sems(
            "rc_in tri_ok lgt_mm lgt_sb lg_ps td_ok te_ok msk_ok pos_ps hot_ok ovf_ok")
        g_mm, g_f32, g_hi, g_lo, e_silu, e_prod, t_ps, t_hi, t_lo, pt1_ps, pt1_sb, ysb_ok, sc_mm, acc_ok = sems(
            "g_mm g_f32 g_hi g_lo e_silu e_prod t_ps t_hi t_lo pt1_ps pt1_sb ysb_ok sc_mm acc_ok")
        v_in = [sem(f"v_in{i}") for i in range(2)]
        v_used, v_hot, v_gps, v_x, v_gu, v_silu, v_prod, v_tps, v_t, v_y, v_sc, v_acc = sems(
            "v_used v_hot v_gps v_x v_gu v_silu v_prod v_tps v_t v_y v_sc v_acc")
        out_done = sem("out_done")

        def most_crowded(eng):
            eng.wait_ge(ovf_ok, 1)
            return eng.value_load(CNT[0:1, NE:NE + 1], min_val=0, max_val=SEQ)

        def second_passes(eng, most, body):
            passes = eng.alloc_register("passes")
            eng.reg_mov(passes, 0)
            with eng.If(most > P):
                with eng.Fori(0, NE) as e:
                    count = eng.value_load(CNT[0:1, bass.ds(e, 1)], min_val=0, max_val=SEQ)
                    with eng.If(count > P):
                        body(e, eng.snap(passes, min_val=0, max_val=3))
                        eng.reg_add(passes, passes, 1)

        def link(eng, s, box, ins):
            box[0] += 1
            ins.then_inc(s, 1)
            eng.wait_ge(s, box[0])

        block = ctx.enter_context(nc.Block())

        def wait_raw(eng, r):
            eng.wait_ge(raw_in[r % RING], RAW_COUNT[r])

        def step_piece(kind, s, w_in2, w_out2):
            if kind == "C":
                return "p (k n) -> p k n", dict(k=2), w_out2[s * FB:(s + 1) * FB, :].rearrange("(k p) n -> p k n", p=P)
            half = "AB".index(kind)
            src = w_in2.rearrange("(k p) (g n) -> p k g n", p=P, g=2)
            return ("p (k g n) -> p k g n", dict(k=4, g=2),
                    src[:, 4 * half:4 * half + 4, :, s * FB:(s + 1) * FB])

        def stream_step(m, steps):
            if m < 2:
                return 0, "AB"[m]
            if m == 3 * steps - 1:
                return steps - 1, "C"
            t, q = divmod(m + 1, 3)
            return (t, "AB"[q]) if q < 2 else (t - 1, "C")

        def unit_source(v):
            if v < V_FFN:
                return step_piece("AB"[v % 2], v // 2, w_glu, None)
            if v < V_MLA:
                t, kind = stream_step(v - V_FFN, FSTEPS)
                return step_piece(kind, t, ffn_in, ffn_out)
            if v < V_MOE:
                m = v - V_MLA
                if m < 3:
                    return "p (k n) -> p k n", dict(n=PROJ), \
                        mla_in.rearrange("(k p) n -> p k n", p=P)[:, 3 * m:min(3 * m + 3, DT), :]
                if m < 6:
                    return "p n -> p n", {}, w_uq[(m - 3) * P:(m - 2) * P, :]
                if m < 8:
                    return "p n -> p n", {}, w_ukv[(m - 6) * P:(m - 5) * P, :]
                return "p (k n) -> p k n", dict(k=2), \
                    w_o[(m - 8) * 2 * P:(m - 7) * 2 * P, :].rearrange("(k p) n -> p k n", p=P)
            t, kind = stream_step(v - V_MOE, MSTEPS * NE)
            e, s = divmod(t, MSTEPS)
            return step_piece(kind, s, moe_in[e], moe_out[e])

        def unit_width(v):
            m = v - V_MLA
            return (3, 3, 2)[m] * PROJ if 0 <= m < 3 else H * QK if 3 <= m < 6 else UNIT

        def moe_at(i, m):
            return i * (6 * MSTEPS) + (V_MOE + m)

        def moe_units(first, last, tau):
            a = 0 if first and tau == 0 else 3 * tau - 1
            return a, a + 1, 3 * tau + (2 if last and tau == 2 * MSTEPS - 1 else 4)

        def wait_raw_moe(eng, i, m):
            if isinstance(i, int):
                return wait_raw(eng, RAW_OF_W[moe_at(i, m)])
            r = RAW_OF_W[moe_at(1, m)]
            grows = RAW_COUNT[r + 6 * MSTEPS] - RAW_COUNT[r]
            eng.wait_ge(raw_in[r % RING], i * grows + (RAW_COUNT[r] - grows))

        def moe_loop(eng, pair):
            pair(0, True, False)
            with eng.Fori(1, NE // 2 - 1) as i:
                pair(i, False, False)
            pair(NE // 2 - 1, False, True)

        def o_chunk(eng, link_, temps, q):
            if q is None:
                lags, sh = slice(L, L + 1), [P, GI, 1, GH]
                g = slice(0, GI)
            else:
                lags, sh = slice(0, L), [P, 4, L, GH]
                g = slice(4 * q, 4 * q + 4)
            cr, ci = [CT[:, c, g, :].unsqueeze(2).broadcast_to(sh) for c in range(2)]
            pw = [PW[:, i, g, lags].unsqueeze(3).broadcast_to(sh) for i in range(4)]
            dst = [O[:, c, g, lags, :] for c in range(2)]
            t0, t1 = [t.rearrange("p (g t h) -> p g t h", g=sh[1], t=sh[2]) for t in temps]
            eng.tensor_tensor(dst[0], cr, pw[0], ALU.mult)
            eng.tensor_tensor(dst[1], ci, pw[2], ALU.mult)
            eng.tensor_tensor(t0, ci, pw[3], ALU.mult)
            link_(eng.tensor_tensor(t1, cr, pw[3], ALU.mult))
            eng.tensor_tensor(dst[0], dst[0], t0, ALU.add)
            return eng.tensor_tensor(dst[1], dst[1], t1, ALU.add)

        def m_blocks(eng, rows):
            eng.wait_ge(m_zero, 1)
            eng.wait_ge(strip_ok, 4)
            for i in rows:
                for c4 in range(4):
                    p0 = 32 * c4 + GH * (c4 % 2)
                    eng.dma_start(M[GH * i:GH * (i + 1), c4:NG:4, GH * i:P], STRIP[p0:p0 + GH, :, 0:(L - i) * GH])\
                        .then_inc(m_in, 16)

        @block.sync
        def _(sp):
            r0 = 0
            for src in (norm_g.rearrange("l i (t p) -> (l i t) p", p=P), d_in.rearrange("(t p) -> t p", p=P),
                        c_in.rearrange("a (t p) -> (a t) p", p=P), q_norm.rearrange("(t p) -> t p", p=P),
                        kv_norm.rearrange("(t p) -> t p", p=P)):
                n = src.shape[0]
                sp.dma_start(ROWS[r0:r0 + n, :], src).then_inc(rows_in, 16)
                r0 += n

            def load(slot, n):
                form, dims, src = unit_source(n)
                dst = RAW[:, slot, 0:unit_width(n)]
                dst = dst.rearrange(form, **dims) if dims else dst
                for g in range(dims.get("g", 1)):
                    part = (dst[:, :, g, :], src[:, :, g, :]) if "g" in dims else (dst, src)
                    sp.dma_start(*part).then_inc(raw_in[slot], 16)

            looped = 6 * MSTEPS - 1
            for r, (kind, n) in enumerate(STREAM[:RAW_OF_W[V_MOE + looped]]):
                if r == RAW_OF_W[RING]:
                    sp.wait_ge(y2_ok, 4)
                    for tau in range(1, L, 2):
                        sp.dma_start(scr_y.rearrange("(g h) t j -> h t g j", h=GH)[:, tau, :, :],
                                     Y2[GH * tau:GH * (tau + 1), :, :, :].rearrange("p a c j -> p (a c) j"))\
                            .then_inc(y_out, 16)
                if r >= RING:
                    k0, n0 = STREAM[r - RING]
                    sp.wait_ge(ada_used if k0 == "ada" else lo_done, n0 + 1)
                if r == RING + 14:
                    m_blocks(sp, range(0, L, 2))
                slot = r % RING
                if kind == "ada":
                    s, kk = divmod(n, 4)
                    src = w_ada[s // 6, 2 * kk * P:2 * (kk + 1) * P, (s % 6) * D:(s % 6 + 1) * D]
                    sp.dma_start(RAW[:, slot, :].rearrange("p (k n) -> p k n", k=2),
                                 src.rearrange("(k p) n -> p k n", p=P)).then_inc(raw_in[slot], 16)
                else:
                    load(slot, n)
            with sp.Fori(1, NE // 2) as i:
                for m in range(-1, looped):
                    sp.wait_ge(lo_done, moe_at(i, m - RING + 1))
                    slot = (RAW_OF_W[V_MOE] + m) % RING
                    tau, q = divmod(m + 1, 3)
                    j, s = divmod(tau - q // 2, MSTEPS)
                    if q < 2:
                        src = moe_in[bass.ds(i * 2 + j, 1), :, :].rearrange("o (k p) (g n) -> p (o k) g n", p=P, g=2)
                        dst = RAW[:, slot, :].rearrange("p (k g n) -> p k g n", k=4, g=2)
                        for g in range(2):
                            sp.dma_start(dst[:, :, g, :], src[:, 4 * q:4 * q + 4, g, s * FB:(s + 1) * FB])\
                                .then_inc(raw_in[slot], 16)
                    else:
                        src = moe_out[bass.ds(i * 2 + j, 1), s * FB:(s + 1) * FB, :].rearrange("o (k p) n -> p (o k) n", p=P)
                        sp.dma_start(RAW[:, slot, :].rearrange("p (k n) -> p k n", k=2), src).then_inc(raw_in[slot], 16)
            sp.wait_ge(lo_done, V_ALL - RING)
            load(RAW_OF_W[V_ALL - 1] % RING, V_ALL - 1)

            def pass_weights(e, k):
                w_e = moe_in[bass.ds(e, 1), :, :].rearrange("o (k p) (g n) -> p (o k) g n", p=P, g=2)
                wo_e = moe_out[bass.ds(e, 1), :, :].rearrange("o (s k p) n -> s p (o k) n", k=2, p=P)
                for s in range(MSTEPS):
                    if s == 0:
                        sp.wait_ge(v_hot, k * 3 + 1)
                    elif s >= 2:
                        sp.wait_ge(v_used, k * MSTEPS + s - 1)
                    for g in range(2):
                        sp.dma_start(VG[:, s % 2, :, g, :], w_e[:, :, g, s * FB:(s + 1) * FB])\
                            .then_inc(v_in[s % 2], 16)
                    sp.dma_start(VDN[:, s % 2, :, :], wo_e[s, :, :, :]).then_inc(v_in[s % 2], 16)

            most = most_crowded(sp)
            sp.wait_ge(lo_done, V_ALL)
            second_passes(sp, most, pass_weights)

        def wait_section_free(eng, s):
            if s in GATES:
                eng.wait_ge(gate_out[GATES.index(s)], 16)
            else:
                eng.wait_ge(mod_ok, sum(1 for i in range(s + 1) if i not in GATES))

        @block.gpsimd
        def _(pool):
            chain = [0]

            def link_(ins):
                link(pool, pch, chain, ins)

            link_(pool.memset(IDENT[:, :], 0.0))
            pool.affine_select(out=IDENT[:, :], in_=IDENT[:, :], compare_op=ALU.not_equal, fill=1.0, base=0,
                               pattern=[[-1, P]], channel_multiplier=1).then_inc(ident_ok, 1)
            for g2 in range(2):
                for c, b in enumerate((b_re, b_im)):
                    pool.dma_start(BN[g2 * NS:(g2 + 1) * NS, c, :, :],
                                   b[g2 * GI:(g2 + 1) * GI, :, :].rearrange("g p h -> p g h")).then_inc(bn_in, 16)
            pool.dma_start(POSI[:, :], pos_in[0, :].rearrange("(t p) -> p t", p=P),
                           allow_slow_non_contiguous=True).then_inc(pos_ld, 16)
            link_(pool.iota(IOTI[:, :], pattern=[[1, P]], base=0, channel_multiplier=0))
            pool.tensor_copy(IOTA[:, :], IOTI[:, :])
            for i in range(HALF):
                pool.memset(INVF[:, i:i + 1], float(np.float32(10000.0) ** np.float32(-i / HALF)))
            pool.memset(EPSC[:, :], EPS).then_inc(iota_ok, 1)

            def section_rows(s):
                if s >= 2:
                    wait_section_free(pool, s - 2)
                l, kind = divmod(s, 6)
                pool.dma_start(BROW[:, s % 2, :], b_ada[l, kind * D:(kind + 1) * D].rearrange("(c n) -> c n", c=4))\
                    .then_inc(bias_in[s % 2], 16)
                pool.dma_start(NROW[:, s % 2, :], norm_g[l, 1 if kind == 2 else 3, :].rearrange("(c n) -> c n", c=4))\
                    .then_inc(bias_in[s % 2], 16)

            def gate_store(s):
                pool.wait_ge(mrow_ok, s + 1)
                pool.dma_start(scr_gate[GATES.index(s), :].rearrange("(c n) -> c n", c=4), MROW[:, s % 2, :])\
                    .then_inc(gate_out[GATES.index(s)], 16)

            section_rows(0)
            section_rows(1)

            pool.wait_ge(pw_ok, 1)
            pool.wait_ge(ct_ok, 2)

            temps = [OTMP[:, i, :] for i in range(2)]
            for q in range(O_ON_POOL):
                link_(o_chunk(pool, link_, temps, q))
            o_chunk(pool, link_, temps, None).then_inc(o_ok, 1)
            section_rows(2)
            pool.wait_ge(o_ok, 2)
            pool.wait_ge(rblk_ok, GI // 2)
            pool.wait_ge(tab_ok, 1)
            pool.memset(M[:, :, :], 0.0).then_inc(m_zero, 1)
            gate_store(2)
            section_rows(3)
            section_rows(4)
            section_rows(5)
            gate_store(5)
            pool.wait_ge(yt_ok, DT)
            pool.wait_ge(gate_out[0], 16)
            pool.dma_start(GROW[:, :], scr_gate[0, :].partition_broadcast(P)).then_inc(gate_in, 16)
            section_rows(6)
            pool.wait_ge(res_ok, TT)
            pool.wait_ge(gate_out[1], 16)
            pool.dma_start(GROW[:, :], scr_gate[1, :].partition_broadcast(P)).then_inc(gate_in, 16)
            for s in range(7, NSEC):
                section_rows(s)
                if s - 1 in GATES:
                    gate_store(s - 1)
            gate_store(NSEC - 1)
            pool.wait_ge(ada_used, 48)
            link_(pool.memset(MASK[:, :], 0.0))
            pool.affine_select(out=MASK[:, P:], in_=MASK[:, P:], compare_op=ALU.is_ge, fill=NEG, base=0,
                               pattern=[[-1, P]], channel_multiplier=1).then_inc(mask_ok, 1)
            pool.wait_ge(o_mm, H)
            pool.dma_start(GROW[:, :], scr_gate[2, :].partition_broadcast(P)).then_inc(gate_in, 16)
            pool.dma_start(WR[:, :, :], w_router.rearrange("(t p) e -> p t e", p=P)).then_inc(rc_in, 16)
            pool.dma_start(BRT[:, :], b_router.partition_broadcast(P)).then_inc(rc_in, 16)
            pool.memset(ONES[:, :], 1.0)
            link_(pool.memset(TRI[:, :], 1.0))
            pool.affine_select(out=TRI[:, :], in_=TRI[:, :], compare_op=ALU.is_gt, fill=0.0, base=0,
                               pattern=[[1, P]], channel_multiplier=-1).then_inc(tri_ok, 1)
            pool.wait_ge(acc_ok, 4 * NE)
            pool.dma_start(GROW[:, :], scr_gate[3, :].partition_broadcast(P)).then_inc(gate_in, 16)

        @block.tensor
        def _(pe):
            mm, tr = nc.tensor.matmul, nc.tensor.transpose

            def mm3(dst, st, mv, first, last):
                mm(dst, st[0], mv[0], start=first, stop=False)
                mm(dst, st[0], mv[1], start=False, stop=False)
                return mm(dst, st[1], mv[0], start=False, stop=last)

            def unit(v, form, **dims):
                w = unit_width(v)
                return [t[:, v % RING, 0:w].rearrange(form, **dims) for t in (HI, LO)]

            def wait_unit(v):
                pe.wait_ge(lo_done, v + 1)

            pe.wait_ge(ident_ok, 1)
            pe.wait_ge(rows_in, 16 * 5)
            tr(PS[:, 2, 0:85], ROWS[0:85, :], IDENT[0:85, 0:85]).then_inc(vec_ps, 1)
            pe.wait_ge(a_in, 48)
            pe.wait_ge(ldt_ok, 1)
            tr(PS[:, 3, 0:96], AROWS[:, :, :].rearrange("a g p -> a (g p)"), IDENT[0:96, 0:96]).then_inc(at_ps, 1)
            pe.wait_ge(cn_in, 64)
            for c in range(2):
                for k in range(4):
                    last = tr(PS[:, c, k * P:(k + 1) * P], CN[:, c, k, :, :].rearrange("a x p -> a (x p)"), IDENT[:, :])
                last.then_inc(ct_ps, 1)

            def ada_bank(s):
                return 4 + s % 2 if s < 6 else 6 + s % 2

            def ada(n):
                s, kk = divmod(n, 4)
                wait_raw(pe, RAW_OF_ADA[n])
                if n == 0:
                    pe.wait_ge(cb_ok, 1)
                if kk == 0 and s >= 2 and s not in (6, 7):
                    old = s - 2
                    pe.wait_ge(wide_ok, old + 1)
                    if old not in GATES:
                        pe.wait_ge(mod_ok, sum(1 for i in range(old + 1) if i not in GATES))
                for k in range(2):
                    for c4 in range(4):
                        last = mm(PS[32 * c4:32 * c4 + 32, ada_bank(s), 0:256], CB[:, 2 * kk + k, :],
                                  RAW[:, RAW_OF_ADA[n] % RING, k * D + c4 * 256:k * D + (c4 + 1) * 256],
                                  start=kk == 0 and k == 0, stop=kk == 3 and k == 1)
                last.then_inc(ada_used, 1)

            def mod_columns(s):
                pe.wait_ge(mrow_ok, s + 1)
                for half in range(2):
                    last = mm(PS[:, ada_bank(s), 256 + half:256 + half + 7:2], MROW[0:4, s % 2, half * P:(half + 1) * P],
                              IDENT[0:4, 0:4], start=True, stop=True)
                last.then_inc(mod_ps, 1)

            def r_round(r):
                for c in range(2):
                    n = 2 * r + c
                    pe.wait_ge(rblk_ok, n + 1)
                    if n >= 2:
                        pe.wait_ge(rt_ok, n - 1)
                    for q in range(4):
                        last = tr(PS[:, 6 + c, q * P:(q + 1) * P],
                                  RBLK[:, c, q, :, :].rearrange("p t h -> p (t h)"), IDENT[:, :])
                    last.then_inc(rt_ps, 1)

            def norm(m, src):
                pe.wait_ge(n_tok, TT * (m + 1))
                for r in range(4):
                    if r >= 2:
                        pe.wait_ge(n_f32, DT * m + 2 * (r - 1))
                    for dt in (2 * r, 2 * r + 1):
                        for tt in range(TT):
                            last = tr(PS[:, 6 + r % 2, (dt % 2) * SEQ + tt * P:(dt % 2) * SEQ + (tt + 1) * P],
                                      src[:, tt, dt * P:(dt + 1) * P], IDENT[:, :])
                    last.then_inc(n_ps, 1)

            for r in range(4):
                ada(2 * r)
                ada(2 * r + 1)
                r_round(r)
            mod_columns(0)
            mod_columns(1)
            pe.wait_ge(rt_ok, 8)
            norm(0, XN0)
            pe.wait_ge(n_f32, DT)
            for r in range(4, 8):
                r_round(r)
            for n in range(8, 12):
                ada(n)
            pe.wait_ge(bb_ok, 1)
            pe.wait_ge(o_ok, 2)
            for g in range(NG):
                g2, gi, c4, gq = g // GI, g % GI, g % 4, g // 4
                half = slice(g2 * NS, (g2 + 1) * NS)
                for c in range(2):
                    last = mm(PS[32 * c4:32 * c4 + 32, gq // 4, (gq % 4) * P:(gq % 4 + 1) * P],
                              BB[half, c, gi - gi % 2:gi - gi % 2 + 2, :].rearrange("p g h -> p (g h)"),
                              O[half, c, gi, 0:L, :].rearrange("p t h -> p (t h)"), start=c == 0, stop=c == 1)
                if g % 16 == 15:
                    last.then_inc(strip_ps, 1)
            for n in range(12, 16):
                ada(n)
            pe.wait_ge(u_in, 16 * L)
            pe.wait_ge(rt_ok, 16)
            pe.wait_ge(strip_ok, 4)
            for c in range(2):
                for gi in range(GI):
                    for g2 in range(2):
                        last = mm(PS[g2 * NS:(g2 + 1) * NS, 2 * c + gi // 16, (gi % 16) * NJ:(gi % 16 + 1) * NJ],
                                  RT[:, c, gi, g2 * NS:(g2 + 1) * NS], U[:, g2 * GI + gi, :], start=True, stop=True)
            last.then_inc(v_ps, 1)
            mod_columns(3)
            for n in range(16, 24):
                ada(n)
            pe.wait_ge(m_in, 16 * 32)
            pe.wait_ge(s_ok, 1)
            for g in range(NG):
                g2, gi, c4, gq = g // GI, g % GI, g % 4, g // 4
                half = slice(g2 * NS, (g2 + 1) * NS)
                dst = PS[32 * c4:32 * c4 + 32, gq // 4, (gq % 4) * P:(gq % 4 + 1) * P]
                mm(dst, U[:, g, :], M[:, g, :], start=True, stop=False)
                for c in range(2):
                    last = mm(dst, S[half, c, gi, :], O[half, c, gi, 1:L + 1, :].rearrange("p t h -> p (t h)"),
                              start=False, stop=c == 1)
                if g % 16 == 15:
                    last.then_inc(y_ps, 1)
            mod_columns(4)
            for q in range(4):
                pe.wait_ge(y1_ok, q + 1)
                if q >= 2:
                    pe.wait_ge(y2_ok, q - 1)
                for i in range(4):
                    last = tr(PS[:, 6 + q % 2, i * P:(i + 1) * P], Y1[:, 4 * q + i, :], IDENT[:, :])
                last.then_inc(y2_ps, 1)

            for n in range(4):
                if n >= 2:
                    pe.wait_ge(glu_ok, TT * (n - 1))
                for half in range(2):
                    v = V_GLU + 2 * n + half
                    wait_unit(v)
                    w = unit(v, "p (k n) -> p k n", k=4)
                    for tt in range(TT):
                        for k in range(4):
                            kt = 4 * half + k
                            if n == 0 and tt == 0:
                                pe.wait_ge(zl_ok, kt + 1)
                            last = mm3(PS[:, 2 * (n % 2) + tt, :], [z[:, kt, tt * P:(tt + 1) * P] for z in (AH, AL)],
                                       [x[:, k, :] for x in w], kt == 0, kt == DT - 1)
                        if tt == 1:
                            last.then_inc(unit_used, 1)
                        elif half == 1:
                            last.then_inc(glu_mm, 1)

            norm(1, TOK)

            def ffn_down(t):
                v = V_FFN + (3 * t + 4 if t < FSTEPS - 1 else 3 * t + 2)
                wait_unit(v)
                w = unit(v, "p (k n) -> p k n", k=2)
                for ft in range(2):
                    f = 2 * t + ft
                    pe.wait_ge(f_lo, f + 1)
                    for tt in range(TT):
                        for dh in range(2):
                            last = mm3(PS[:, 2 * tt + dh, :], [x[:, f % 4, tt * P:(tt + 1) * P] for x in (GTH, GTL)],
                                       [x[:, ft, dh * 512:(dh + 1) * 512] for x in w], f == 0, f == 2 * FSTEPS - 1)
                last.then_inc(unit_used, 1)

            pe.wait_ge(glu_ok, 8)
            for t in range(FSTEPS):
                va = V_FFN + 3 * t - (1 if t else 0)
                wait_unit(va)
                wait_unit(va + 1)
                wa, wb = [unit(v, "p (k g n) -> p k g n", k=4, g=2) for v in (va, va + 1)]
                for ft in range(2):
                    f = 2 * t + ft
                    if f >= 2:
                        pe.wait_ge(f_prod, f - 1)
                    for g in range(2):
                        for kt in range(DT):
                            w = wa if kt < 4 else wb
                            if f == 0 and g == 0:
                                pe.wait_ge(n_lo, kt + 1)
                            last = mm3(PS[:, 4 + f % 2, g * SEQ:(g + 1) * SEQ],
                                       [x[:, kt % 4, g, ft * P:(ft + 1) * P] for x in w],
                                       [x[:, kt, :] for x in (AH, AL)], kt == 0, kt == DT - 1)
                    last.then_inc(*((unit_used, 2) if ft else (f_mm, 1)))
                    if ft == 0 and t and t % 2 == 0 and 5 + t // 2 not in GATES:
                        mod_columns(5 + t // 2)
                if t:
                    ffn_down(t - 1)
                for n in range(24 + (2 + 2 * t if t else 0), 28 + 2 * t):
                    ada(n)
            ffn_down(FSTEPS - 1)

            norm(2, TOK)
            pe.wait_ge(res_ok, 2 * TT)
            cols = ((0, QR), (QR, PROJ))
            for m in range(3):
                v = V_MLA + m
                wait_unit(v)
                w = unit(v, "p (k n) -> p k n", n=PROJ)
                for tt in range(TT):
                    for i, (c0, c1) in enumerate(cols):
                        for kt in range(3 * m, min(3 * m + 3, DT)):
                            if tt == 0 and i == 0:
                                pe.wait_ge(n_lo, DT + kt + 1)
                            last = mm3(PS[:, 2 * tt + i, 0:c1 - c0], [x[:, kt, tt * P:(tt + 1) * P] for x in (AH, AL)],
                                       [x[:, kt - 3 * m, c0:c1] for x in w], kt == 0, kt == DT - 1)
                last.then_inc(unit_used, 1)
            pe.wait_ge(p_nrm, TT)
            for i in range(5):
                for tt in range(TT):
                    last = tr(PS[:, (6, 7, 5)[i // 2], (i % 2) * SEQ + tt * P:(i % 2) * SEQ + (tt + 1) * P],
                              PR[:, tt, i * P:(i + 1) * P], IDENT[:, :])
                last.then_inc(p_ps, 1)
            pe.wait_ge(p_lo, 5)
            for k in range(3):
                v = V_MLA + 3 + k
                wait_unit(v)
                w = unit(v, "p n -> p n")
                for tt in range(TT):
                    for b in range(3):
                        last = mm3(PS[:, 3 * tt + b, :], [x[:, k, tt * P:(tt + 1) * P] for x in (CQH, CQL)],
                                   [x[:, b * 512:(b + 1) * 512] for x in w], k == 0, k == 2)
                last.then_inc(unit_used, 1)
            for k in range(2):
                v = V_MLA + 6 + k
                wait_unit(v)
                w = unit(v, "p n -> p n")
                for tt in range(TT):
                    if k == 0:
                        pe.wait_ge(q_sb, (2, 6)[tt])
                    for b in range(4):
                        last = mm3(PS[:, (6 + 4 * tt + b) % 8, :], [x[:, 3 + k, tt * P:(tt + 1) * P] for x in (CQH, CQL)],
                                   [x[:, b * 512:(b + 1) * 512] for x in w], k == 0, k == 1)
                last.then_inc(unit_used, 1)
            pe.wait_ge(k_rope, 2 * TT)
            pe.wait_ge(q_rope, TT)
            pe.wait_ge(kf_ok, 8)
            pe.wait_ge(vv_ok, 8)

            def head_transpose(h):
                if h >= 2:
                    pe.wait_ge(qk_sb, h - 1)
                for i, src in enumerate((Q, KF)):
                    for tt in range(TT):
                        last = tr(PS[0:QK, h % 2, (2 * i + tt) * P:(2 * i + tt + 1) * P], src[:, tt, h, :], IDENT[:, :])
                last.then_inc(qk_ps, 1)

            def head_scores(h):
                b = h % 2
                pe.wait_ge(qk_sb, h + 1)
                if h >= 2:
                    pe.wait_ge(s_max, h - 1)
                mm(PS[:, 2 + b, 0:P], QKT[:, b, 0, 0:P], QKT[:, b, 1, 0:P], start=True, stop=True)
                mm(PS[:, 2 + b, P:3 * P], QKT[:, b, 0, P:], QKT[:, b, 1, :], start=True, stop=True).then_inc(s_mm, 1)

            def head_probs(h):
                b = h % 2
                pe.wait_ge(pn_ok, h + 1)
                if h >= 2:
                    pe.wait_ge(pt_sb, h - 1)
                for i in range(3):
                    last = tr(PS[:, 4 + b, i * P:(i + 1) * P], PB[:, b, i * P:(i + 1) * P], IDENT[:, :])
                last.then_inc(pt_ps, 1)

            def head_values(h):
                b, pair = h % 2, h // 2
                pe.wait_ge(pt_sb, h + 1)
                if b == 0 and pair >= 2:
                    pe.wait_ge(o_lo, pair - 1)
                dst = PS[b * VD:(b + 1) * VD, 6 + pair % 2, 0:SEQ]
                mm(dst, VV[:, 0, h, :], PTB[:, b, 0:SEQ], start=True, stop=False)
                mm(dst[:, P:], VV[:, 1, h, :], PTB[:, b, SEQ:], start=False, stop=True).then_inc(o_mm, 1)

            for i in range(H + 3):
                if i < H:
                    head_transpose(i)
                if 0 <= i - 1 < H:
                    head_scores(i - 1)
                if 0 <= i - 2 < H:
                    head_probs(i - 2)
                if 0 <= i - 3 < H:
                    head_values(i - 3)
            pe.wait_ge(o_lo, H // 2)
            for m in range(4):
                v = V_MLA + 8 + m
                wait_unit(v)
                w = unit(v, "p (k n) -> p k n", k=2)
                for tt in range(TT):
                    for dh in range(2):
                        for k in range(2):
                            kt = 2 * m + k
                            last = mm3(PS[:, 2 * tt + dh, :], [x[:, kt, tt * P:(tt + 1) * P] for x in (OTH, OTL)],
                                       [x[:, k, dh * 512:(dh + 1) * 512] for x in w], kt == 0, kt == DT - 1)
                last.then_inc(unit_used, 1)

            norm(3, TOK)
            pe.wait_ge(n_f32, 4 * DT)
            pe.wait_ge(rc_in, 32)
            for kt in range(DT):
                last = mm(PS[0:NE, 4, 0:SEQ], WR[:, kt, :], H32[:, kt, :], start=kt == 0, stop=kt == DT - 1)
            last.then_inc(lgt_mm, 1)
            pe.wait_ge(lgt_sb, 1)
            for tt in range(TT):
                last = mm(PS[:, 5, tt * NE:(tt + 1) * NE], LGT[:, tt * P:(tt + 1) * P], IDENT[0:NE, 0:NE],
                          start=True, stop=True)
            last.then_inc(lg_ps, 1)
            pe.wait_ge(tri_ok, 1)
            pe.wait_ge(msk_ok, 1)
            mm(PS[:, 4, 0:NE], TRI[:, :], MSK[:, 0, :], start=True, stop=True)
            mm(PS[:, 4, NE:2 * NE], ONES[:, :], MSK[:, 0, :], start=True, stop=False)
            mm(PS[:, 4, NE:2 * NE], TRI[:, :], MSK[:, 1, :], start=False, stop=True)
            mm(PS[:, 4, 2 * NE:3 * NE], ONES[:, :], MSK[:, 0, :], start=True, stop=False)
            mm(PS[:, 4, 2 * NE:3 * NE], ONES[:, :], MSK[:, 1, :], start=False, stop=True).then_inc(pos_ps, 1)

            def gather(e, b, r, first=False):
                if r:
                    pe.wait_ge(g_f32, e * DT + 4)
                elif not first:
                    pe.wait_ge(acc_ok, e * 4 - 4)
                elif isinstance(e, int) and e:
                    pe.wait_ge(g_f32, DT)
                pe.wait_ge(hot_ok, e * 2 + 2)
                for q in range(4):
                    dt = 4 * r + q
                    for tt in range(TT):
                        last = mm(PS[:, 7, q * P:(q + 1) * P], TOK[:, tt, dt * P:(dt + 1) * P], ONE[:, b, tt, :],
                                  start=tt == 0, stop=tt == TT - 1)
                last.then_inc(g_mm, 1)

            def slot_rows(e, b, last_expert):
                if last_expert:
                    pe.wait_ge(acc_ok, e * 4)
                else:
                    pe.wait_ge(g_f32, e * DT + 2 * DT)
                for tt in range(TT):
                    tr(PS[:, 7, tt * P:(tt + 1) * P], ONE[:, b, tt, :], IDENT[:, :])
                for tt in range(TT):
                    last = mm(PS[:, 7, SEQ:SEQ + 1], ONE[:, b, tt, :], HOT[:, b, 1, tt:tt + 1], start=tt == 0, stop=tt == 1)
                last.then_inc(pt1_ps, 1)

            def scatter(e, i, bank=7):
                tt, dh = divmod(i, 2)
                if i == 0:
                    pe.wait_ge(pt1_sb, e + 1)
                    pe.wait_ge(ysb_ok, e + 1)
                elif i == 3 and bank != 7:
                    pe.wait_ge(acc_ok, e * 4 + 1)
                elif bank == 7:
                    pe.wait_ge(acc_ok, e * 4 + i)
                mm(PS[:, bank, :], PT[:, tt * P:(tt + 1) * P], YSB[:, dh * 512:(dh + 1) * 512], start=True, stop=True)\
                    .then_inc(sc_mm, 1)

            def expert_transpose(i, tau, first):
                t = i * (2 * MSTEPS) + tau
                pe.wait_ge(e_prod, t + 1)
                if not (first and tau == 0):
                    pe.wait_ge(t_lo, t)
                for ft in range(2):
                    last = tr(PS[:, 6, ft * P:(ft + 1) * P], EPR[:, tau % 2, ft * P:(ft + 1) * P], IDENT[:, :])
                last.then_inc(t_ps, 1)

            def unit_moe(m, form, **dims):
                return [t[:, (V_MOE + m) % RING, :].rearrange(form, **dims) for t in (HI, LO)]

            def expert_down(i, tau, first, last_pair):
                j, s = divmod(tau, MSTEPS)
                m = moe_units(first, last_pair, tau)[2]
                pe.wait_ge(lo_done, moe_at(i, m) + 1)
                pe.wait_ge(t_lo, i * (2 * MSTEPS) + tau + 1)
                if s == 0 and not first:
                    pe.wait_ge(ysb_ok, i * 2 + j - 1)
                w = unit_moe(m, "p (k n) -> p k n", k=2)
                for dh in range(2):
                    for ft in range(2):
                        last = mm3(PS[:, 2 * (j % 2) + dh, :], [x[:, tau % 2, ft, :] for x in (EGH, EGL)],
                                   [x[:, ft, dh * 512:(dh + 1) * 512] for x in w],
                                   s == 0 and ft == 0, s == MSTEPS - 1 and ft == 1)
                last.then_inc(unit_used, 1)

            def expert_pair(i, first, last_pair):
                for tau in range(2 * MSTEPS):
                    j, s = divmod(tau, MSTEPS)
                    e = i * 2 + j
                    start, end = first and j == 0, last_pair and j == 1
                    a, b, _ = moe_units(first, last_pair, tau)
                    if not (first and tau < 2):
                        pe.wait_ge(e_prod, i * (2 * MSTEPS) + tau - 1)
                    for half, m in enumerate((a, b)):
                        pe.wait_ge(lo_done, moe_at(i, m) + 1)
                        if s == 0:
                            pe.wait_ge(g_lo, e * 2 + half + 1)
                        w = unit_moe(m, "p (k n) -> p k n", k=4)
                        for k in range(4):
                            kt = 4 * half + k
                            last = mm3(PS[:, 4 + tau % 2, :], [x[:, j, kt, :] for x in (XEH, XEL)],
                                       [x[:, k, :] for x in w], kt == 0, kt == DT - 1)
                        last.then_inc(unit_used, 1)
                        if half == 0 and not (first and tau == 0):
                            expert_transpose(i, tau - 1, first)
                    if s == 0 and not start:
                        slot_rows(e - 1, 1 - j, False)
                    if 1 <= s <= 4 and not start:
                        scatter(e - 1, s - 1)
                    if s >= 5 and not end:
                        gather(e + 1, 1 - j, s - 5, first=start)
                    if not (first and tau == 0):
                        expert_down(i, tau - 1, first, last_pair)

            gather(0, 0, 0, first=True)
            gather(0, 0, 1)
            most = most_crowded(pe)
            moe_loop(pe, expert_pair)
            slot_rows(NE - 1, 1, True)
            expert_transpose(NE // 2 - 1, 2 * MSTEPS - 1, False)
            expert_down(NE // 2 - 1, 2 * MSTEPS - 1, False, True)
            for i in range(4):
                scatter(NE - 1, i, bank=4 + i % 3)

            def second_pass(e, k):
                pe.wait_ge(v_hot, k * 3 + 3)
                for dt in range(DT):
                    for tt in range(TT):
                        last = mm(PS[:, 6 + dt // 4, (dt % 4) * P:(dt % 4 + 1) * P], TOK[:, tt, dt * P:(dt + 1) * P],
                                  VH[:, 0, tt, :], start=tt == 0, stop=tt == TT - 1)
                for tt in range(TT):
                    last = tr(PS[:, 5, tt * P:(tt + 1) * P], VH[:, 1, tt, :], IDENT[:, :])
                last.then_inc(v_gps, 1)
                pe.wait_ge(v_x, k + 1)
                for s in range(MSTEPS):
                    pe.wait_ge(v_in[s % 2], k * (48 * (4, 3)[s % 2]) + 48 * (s // 2 + 1))
                    for kt in range(DT):
                        last = mm(PS[:, 4 + s % 2, :], VX[:, kt, :], VG[:, s % 2, kt, :, :].rearrange("p g n -> p (g n)"),
                                  start=kt == 0, stop=kt == DT - 1)
                    last.then_inc(v_gu, 1)
                    pe.wait_ge(v_prod, k * MSTEPS + s + 1)
                    for ft in range(2):
                        last = tr(PS[:, 6 + s % 2, ft * P:(ft + 1) * P], EPR[:, s % 2, ft * P:(ft + 1) * P], IDENT[:, :])
                    last.then_inc(v_tps, 1)
                    pe.wait_ge(v_t, k * MSTEPS + s + 1)
                    for dh in range(2):
                        for ft in range(2):
                            last = mm(PS[:, dh, :], VT[:, s % 2, ft, :], VDN[:, s % 2, ft, dh * 512:(dh + 1) * 512],
                                      start=s == 0 and ft == 0, stop=s == MSTEPS - 1 and ft == 1)
                    last.then_inc(v_used, 1)
                pe.wait_ge(v_y, k + 1)
                for i in range(4):
                    last = mm(PS[:, 2 + i, :], PT[:, (i // 2) * P:(i // 2 + 1) * P], VY[:, (i % 2) * 512:(i % 2 + 1) * 512],
                              start=True, stop=True)
                last.then_inc(v_sc, 1)

            pe.wait_ge(acc_ok, 4 * NE)
            second_passes(pe, most, second_pass)
        @block.scalar
        def _(act):
            chain = [0]

            def link_(ins):
                link(act, ach, chain, ins)

            af, cp = nc.scalar.activation, ACT.Copy
            done = [0]

            def split_to(v_end):
                while done[0] < v_end:
                    v = done[0]
                    slot, w = v % RING, unit_width(v)
                    wait_raw(act, RAW_OF_W[v])
                    if v >= RING:
                        act.wait_ge(unit_used, v - RING + 1)
                    af(HI[:, slot, 0:w], RAW[:, RAW_OF_W[v] % RING, 0:w], cp).then_inc(hi_done, 1)
                    done[0] += 1

            act.dma_start(LDT[64:96, :], log_dt.rearrange("(x g) -> g x", x=2),
                          allow_slow_non_contiguous=True).then_inc(a_in, 16)
            for i, a in enumerate((a_re, a_im)):
                act.dma_start(AROWS[32 * i:32 * i + 32, :, :], a.rearrange("(x g) p -> g x p", x=2)).then_inc(a_in, 16)
            for c, cc in enumerate((c_re, c_im)):
                for x in range(2):
                    act.dma_start(CN[:, c, :, x, :], cc[x * GI:(x + 1) * GI, :, :]
                                  .rearrange("(k g) h p -> (g h) k p", k=4)).then_inc(cn_in, 16)
            act.dma_start(XN0[:, :, :], x_in[0].rearrange("(t p) n -> p t n", p=P)).then_inc(x_ld, 16)

            act.wait_ge(at_ok, 1)
            af(SM[:, 0, :], AT[:, 64:96], ACT.Exp).then_inc(dt_ok, 1)
            act.wait_ge(tre_ok, 1)
            af(SM[:, 18, :], SM[:, 1, :], ACT.Exp)
            af(SM[:, 19, :], SM[:, 1, :], ACT.Tanh, scale=0.5)
            af(SM[:, 20, :], SM[:, 1, :], ACT.Exp, scale=float(L)).then_inc(fun_ok, 1)
            act.wait_ge(vec_ok, 1)
            af(ST[:, 24:32], VEC[:, 72:80], ACT.Silu).then_inc(cact_ok, 1)
            act.wait_ge(ang_ok, 1)
            af(SM[:, 13:18, :], SM[:, 3:8, :], ACT.Sin).then_inc(fun_ok, 1)
            for c in range(2):
                act.wait_ge(ct_ps, c + 1)
                af(CT[:, c, :, :].rearrange("p g h -> p (g h)"), PS[:, c, :], cp).then_inc(ct_ok, 1)

            def wide(s):
                act.wait_ge(ada_used, 4 * (s + 1))
                if s >= 2:
                    act.wait_ge(row_in[s % 2], 16 * (s // 2))
                af(WIDE[:, s % 2, :], PS[:, (4 if s < 6 else 6) + s % 2, 0:256], cp).then_inc(wide_ok, 1)
                act.wait_ge(wide_ok, s + 1)
                if s >= 2:
                    wait_section_free(act, s - 2)
                act.dma_start(MROW[:, s % 2, :], WIDE[0:P:32, s % 2, :]).then_inc(row_in[s % 2], 16)

            def rt_copy(n):
                act.wait_ge(rt_ps, n + 1)
                af(RT[:, n % 2, 4 * (n // 2):4 * (n // 2) + 4, :].rearrange("p g s -> p (g s)"), PS[:, 6 + n % 2, :], cp)\
                    .then_inc(rt_ok, 1)

            def norm_stats(m, src, junk):
                for tt in range(TT):
                    if m:
                        act.wait_ge(res_ok, (m - 1) * TT + tt + 1)
                    last = af(junk[:, tt, :], src[:, tt, :], ACT.Square, accum_out=ST[:, tt:tt + 1])
                last.then_inc(n_ss, 1)
                act.wait_ge(n_ss, m + 1)
                af(ST[:, 6:8], ST[:, 0:2], ACT.Sqrt, bias=EPSC[:, :], scale=1.0 / D).then_inc(n_rt, 1)

            def norm_hi(m):
                for dt in range(DT):
                    act.wait_ge(n_f32, DT * m + dt + 1)
                    af(AH[:, dt, :], H32[:, dt, :], cp).then_inc(n_hi, 1)

            act.wait_ge(x_ld, 16)
            act.wait_ge(iota_ok, 1)
            norm_stats(0, XN0, JUNK0)
            for n in range(8):
                rt_copy(n)
                if n == 3:
                    wide(0)
            wide(1)
            for dt in range(DT):
                act.wait_ge(n_f32, dt + 1)
                act.dma_start(scr_u.rearrange("(a p) t j -> p a t j", p=P)[:, dt, :, :], UT[:, dt, :, :]).then_inc(u_out, 16)
            for n in range(8, 16):
                rt_copy(n)
            wide(2)
            for q in range(4):
                act.wait_ge(strip_ps, q + 1)
                af(STRIP[:, 4 * q:4 * q + 4, :].rearrange("p a n -> p (a n)"), PS[:, q, :], cp).then_inc(strip_ok, 1)
            act.wait_ge(u_out, 16 * DT)
            for tau in range(L):
                act.dma_start(U[GH * tau:GH * (tau + 1), :, :], scr_u.rearrange("(g h) t j -> h t g j", h=GH)[:, tau, :, :])\
                    .then_inc(u_in, 16)
            m_blocks(act, range(1, L, 2))
            wide(3)
            wide(4)
            wide(5)
            for q in range(4):
                act.wait_ge(y_ps, q + 1)
                af(Y1[:, 4 * q:4 * q + 4, :].rearrange("p a n -> p (a n)"), PS[:, q, :], cp).then_inc(y1_ok, 1)
            for q in range(4):
                act.wait_ge(y2_ps, q + 1)
                af(Y2[:, 4 * q:4 * q + 4, :, :].rearrange("p a c j -> p (a c j)"), PS[:, 6 + q % 2, :], cp).then_inc(y2_ok, 1)
            act.wait_ge(y2_ok, 4)
            for tau in range(0, L, 2):
                act.dma_start(scr_y.rearrange("(g h) t j -> h t g j", h=GH)[:, tau, :, :],
                              Y2[GH * tau:GH * (tau + 1), :, :, :].rearrange("p a c j -> p (a c) j")).then_inc(y_out, 16)
            act.dma_start(X[:, :, :], x_in[0].rearrange("(t p) n -> p t n", p=P)).then_inc(x_ld, 16)
            split_to(2)
            act.wait_ge(y_out, 16 * L)
            act.dma_start(YT[:, :, :, :], scr_y.rearrange("(a p) t j -> p a t j", p=P)).then_inc(yt_in, 16)
            split_to(4)
            for dt in range(DT):
                act.wait_ge(yt_ok, dt + 1)
                link_(af(H32[:, dt, :].rearrange("p (j t) -> p t j", t=L), YT[:, dt, :, :], ACT.Gelu_apprx_tanh))
                af(AH[:, dt, :], H32[:, dt, :], cp).then_inc(zh_ok, 1)
            split_to(6)
            for n in range(4):
                for tt in range(TT):
                    act.wait_ge(*((glu_mm, n + 1) if tt == 0 else (unit_used, 2 * n + 2)))
                    if n >= 2:
                        act.wait_ge(glu_ok, TT * (n - 1))
                    af(SG[:, n % 2, tt, :], PS[:, 2 * (n % 2) + tt, FB:], ACT.Sigmoid).then_inc(sig_ok, 1)
                split_to(min(8 + 2 * n, V_FFN + 4))
            split_to(V_FFN + 4)

            def sqrt_ahead(n):
                af(ST[:, 20 + n:21 + n], EPSC[:, :], ACT.Sqrt)

            def residual_stats(n, pieces):
                for i, src in enumerate(pieces):
                    last = af(RES[:, i, :], src, ACT.Square, accum_out=ST[:, 10 + i:11 + i])
                last.then_inc(r_ss, 1)
                act.wait_ge(r_sum, n + 1)
                af(ST[:, 16:18], ST[:, 14:16], ACT.Sqrt, bias=EPSC[:, :], scale=1.0 / D).then_inc(r_rt, 1)

            sqrt_ahead(1)
            act.wait_ge(glu_ok, 8)
            residual_stats(0, [TOK[:, i // 2, (i % 2) * 512:(i % 2 + 1) * 512] for i in range(4)])
            norm_stats(1, X, JUNK)
            norm_hi(1)
            act.wait_ge(n_lo, DT)
            for t in range(FSTEPS):
                va = V_FFN + 3 * t - (1 if t else 0)
                for ft in range(2):
                    f = 2 * t + ft
                    split_to(va + 4 + ft if t else V_FFN + 3 + ft)
                    act.wait_ge(*((unit_used, va + 2) if ft else (f_mm, t + 1)))
                    if f >= 4:
                        act.wait_ge(f_prod, f - 3)
                    af(FS[:, f % 4, :], PS[:, 4 + f % 2, 0:SEQ], ACT.Silu).then_inc(f_silu, 1)
                    if ft == 0 and t:
                        split_to(va + 5)
                    act.wait_ge(f_prod, f + 1)
                    if f >= 4:
                        act.wait_ge(unit_used, V_FFN + 3 * (t - 2) + 5)
                    af(GTH[:, f % 4, :], FP[:, f % 4, :], cp).then_inc(f_hi, 1)
                split_to(va + 6 if t else V_FFN + 5)
                if t % 2 == 0:
                    wide(6 + t // 2)
            sqrt_ahead(2)
            act.wait_ge(unit_used, V_MLA)
            residual_stats(1, [PS[:, i, :] for i in range(4)])
            norm_stats(2, X, JUNK)
            act.dma_start(scr_x.rearrange("(t p) n -> p t n", p=P), X[:, :, :]).then_inc(x_out, 16)
            norm_hi(2)
            split_to(V_MLA + 6)
            act.wait_ge(cs_arg, 1)
            af(CS[:, 1, :, :], ROT[:, 2, :, :], ACT.Sin)
            af(CS[:, 0, :, :], ROT[:, 3, :, :], ACT.Sin).then_inc(cs_ok, 1)
            act.wait_ge(unit_used, V_MLA + 3)
            for tt in range(TT):
                af(PR[:, tt, 0:QR], PS[:, 2 * tt, 0:QR], cp)
                af(PR[:, tt, QR:], PS[:, 2 * tt + 1, 0:PROJ - QR], cp)
            for tt in range(TT):
                af(RES[:, 2 * tt, 0:QR], PS[:, 2 * tt, 0:QR], ACT.Square, accum_out=ST[:, tt:tt + 1])
                last = af(RES[:, 2 * tt + 1, 0:KR], PS[:, 2 * tt + 1, 0:KR], ACT.Square, accum_out=ST[:, 2 + tt:3 + tt])
            last.then_inc(p_sb, 1)
            act.wait_ge(p_sb, 1)
            af(ST[:, 4:6], ST[:, 0:2], ACT.Sqrt, bias=EPSC[:, :], scale=1.0 / QR)
            af(ST[:, 6:8], ST[:, 2:4], ACT.Sqrt, bias=EPSC[:, :], scale=1.0 / KR).then_inc(p_rt, 1)
            for i in range(5):
                act.wait_ge(p_f32, i + 1)
                af(CQH[:, i, :], C32[:, i, :], cp).then_inc(p_hi, 1)
            split_to(V_MLA + 8)
            act.wait_ge(unit_used, V_MLA + 6)
            act.wait_ge(x_out, 16)
            for tt in range(TT):
                if tt == 1:
                    act.wait_ge(k_rope, 2 * TT)
                for b in range(3):
                    af(Q[:, tt, :, :].rearrange("p h d -> p (h d)")[:, b * 512:(b + 1) * 512], PS[:, 3 * tt + b, :], cp)\
                        .then_inc(q_sb, 1)
            split_to(V_MLA + 9)
            act.wait_ge(unit_used, V_MLA + 8)
            for b in range(4):
                kv = PS[:, (6 + b) % 8, :].rearrange("p (h d) -> p h d", h=4)
                af(KF[:, 0, 4 * b:4 * b + 4, 0:NOPE], kv[:, :, 0:NOPE], cp).then_inc(kf_ok, 1)
                af(VV[:, 0, 4 * b:4 * b + 4, :], kv[:, :, NOPE:], cp).then_inc(vv_ok, 1)
            split_to(V_MLA + 12)
            for i in range(H + 3):
                if i < H:
                    act.wait_ge(qk_ps, i + 1)
                    if i >= 2:
                        act.wait_ge(s_mm, i - 1)
                    af(QKT[:, i % 2, :, :].rearrange("p a s -> p (a s)"), PS[0:QK, i % 2, :], cp).then_inc(qk_sb, 1)
                h = i - 1
                if 0 <= h < H:
                    b = h % 2
                    act.wait_ge(s_max, h + 1)
                    for tt in range(TT):
                        pr = PB[:, b, 0:P] if tt == 0 else PB[:, b, P:]
                        last = af(pr, pr, ACT.Exp, bias=ST[:, 4 + 2 * b + tt:5 + 2 * b + tt], scale=SCALE,
                                  accum_out=ST[:, 8 + 2 * b + tt:9 + 2 * b + tt])
                    last.then_inc(e_ok, 1)
                h = i - 2
                if 0 <= h < H:
                    act.wait_ge(pt_ps, h + 1)
                    if h >= 2:
                        act.wait_ge(o_mm, h - 1)
                    af(PTB[:, h % 2, :], PS[:, 4 + h % 2, 0:384], cp).then_inc(pt_sb, 1)
                h = i - 3
                if h >= 0 and h % 2:
                    act.wait_ge(o_mm, h + 1)
                    af(OTH[:, h // 2, :], PS[:, 6 + (h // 2) % 2, 0:SEQ], cp).then_inc(o_hi, 1)
            act.dma_start(X[:, :, :], scr_x.rearrange("(t p) n -> p t n", p=P)).then_inc(x_ld, 16)
            split_to(V_MOE + 2)
            sqrt_ahead(3)
            act.wait_ge(unit_used, V_MOE)
            residual_stats(2, [PS[:, i, :] for i in range(4)])
            norm_stats(3, X, JUNK)
            act.wait_ge(lgt_mm, 1)
            af(LGT[:, :], PS[0:NE, 4, 0:SEQ], cp).then_inc(lgt_sb, 1)
            act.wait_ge(td_ok, 1)
            af(WT[:, 1, :], WT[:, 0, :], ACT.Exp).then_inc(te_ok, 1)

            def gather_columns(e, b, r, first=False):
                act.wait_ge(g_mm, e * 2 + r + 1)
                if r == 0 and not first:
                    act.wait_ge(sc_mm, e * 4 - 4)
                for q in range(4):
                    scale, shift = MOD[:, 10, 4 * r + q:4 * r + q + 1], MOD[:, 9, 4 * r + q:4 * r + q + 1]
                    af(XE32[:, 4 * r + q, :], PS[:, 7, q * P:(q + 1) * P], ACT.Identity, bias=shift, scale=scale)\
                        .then_inc(g_f32, 1)
                act.wait_ge(g_f32, e * DT + 4 * r + 4)
                af(XEH[:, b, 4 * r:4 * r + 4, :].rearrange("p a s -> p (a s)"),
                   XE32[:, 4 * r:4 * r + 4, :].rearrange("p a s -> p (a s)"), cp).then_inc(g_hi, 1)

            def weighted_rows(e, b, first, last_expert):
                act.wait_ge(unit_used, e * (3 * MSTEPS) + (V_MOE + 3 * MSTEPS + (0 if last_expert else 2)))
                act.wait_ge(pt1_sb, e + 1)
                act.wait_ge(g_lo, e * 2 + (2 if last_expert else 4))
                if not first:
                    act.wait_ge(sc_mm, e * 4)
                af(YSB[:, :], PS[:, 2 * b:2 * b + 2, :].rearrange("p a n -> p (a n)"), cp,
                   scale=WSL[:, 0:1]).then_inc(ysb_ok, 1)

            def slot_rows(e, first):
                act.wait_ge(pt1_ps, e + 1)
                if not first:
                    act.wait_ge(sc_mm, e * 4)
                af(PT[:, :], PS[:, 7, 0:SEQ], cp)
                af(WSL[:, 0:1], PS[:, 7, SEQ:SEQ + 1], cp).then_inc(pt1_sb, 1)

            def split_moe(i, m):
                wait_raw_moe(act, i, m)
                act.wait_ge(unit_used, moe_at(i, m) - RING + 1)
                af(HI[:, (V_MOE + m) % RING, :], RAW[:, (RAW_OF_W[V_MOE] + m) % RING, :], cp).then_inc(hi_done, 1)

            def products_hi(i, tau, first):
                t = i * (2 * MSTEPS) + tau
                act.wait_ge(t_ps, t + 1)
                if not (first and tau < 2):
                    act.wait_ge(unit_used, moe_at(i, moe_units(first, False, tau - 2)[2]) + 1)
                af(EGH[:, tau % 2, :, :].rearrange("p a s -> p (a s)"), PS[:, 6, 0:2 * P], cp).then_inc(t_hi, 1)

            def expert_pair(i, first, last_pair):
                for tau in range(2 * MSTEPS):
                    j, s = divmod(tau, MSTEPS)
                    e = i * 2 + j
                    start, end = first and j == 0, last_pair and j == 1
                    up_next = not (last_pair and tau == 2 * MSTEPS - 1)
                    na, nb, _ = moe_units(first, last_pair, tau + 1)
                    if up_next:
                        split_moe(i, na)
                    if s == 1 and not start:
                        weighted_rows(e - 1, 1 - j, first and j == 1, False)
                    if not (first and tau == 0):
                        products_hi(i, tau - 1, first)
                    if up_next:
                        split_moe(i, nb)
                    split_moe(i, moe_units(first, last_pair, tau)[2])
                    act.wait_ge(unit_used, moe_at(i, moe_units(first, last_pair, tau)[1]) + 1)
                    if not (first and tau < 2):
                        act.wait_ge(e_prod, i * (2 * MSTEPS) + tau - 1)
                    af(ESI[:, tau % 2, :], PS[:, 4 + tau % 2, 0:FB], ACT.Silu).then_inc(e_silu, 1)
                    if s == 0 and not start:
                        slot_rows(e - 1, first and j == 1)
                    if s >= 5 and not end:
                        gather_columns(e + 1, 1 - j, s - 5, first=start)

            gather_columns(0, 0, 0, first=True)
            gather_columns(0, 0, 1)
            most = most_crowded(act)
            moe_loop(act, expert_pair)
            slot_rows(NE - 1, False)
            products_hi(NE // 2 - 1, 2 * MSTEPS - 1, False)
            weighted_rows(NE - 1, 1, False, True)

            def second_pass(e, k):
                for s in range(MSTEPS):
                    act.wait_ge(v_gu, k * MSTEPS + s + 1)
                    af(ESI[:, s % 2, :], PS[:, 4 + s % 2, 0:FB], ACT.Silu).then_inc(v_silu, 1)
                act.wait_ge(v_used, k * MSTEPS + MSTEPS)
                af(VY[:, :], PS[:, 0:2, :].rearrange("p a n -> p (a n)"), cp).then_inc(v_y, 1)
                act.wait_ge(v_acc, k + 1)

            second_passes(act, most, second_pass)
            sqrt_ahead(4)
            residual_stats_acc = [YACC[:, i // 2, (i % 2) * 512:(i % 2 + 1) * 512] for i in range(4)]
            act.wait_ge(acc_ok, 4 * NE)
            residual_stats(3, residual_stats_acc)
            for tt in range(TT):
                act.wait_ge(res_ok, 3 * TT + tt + 1)
                act.dma_start(out[0, tt * P:(tt + 1) * P, :], X[:, tt, :]).then_inc(out_done, 16)
            act.wait_ge(out_done, 16 * TT)
            act.wait_ge(u_out, 16 * DT)
            act.wait_ge(y_out, 16 * L)
            act.wait_ge(x_out, 16)
            for g in gate_out:
                act.wait_ge(g, 16)

        @block.vector
        def _(dve):
            chain = [0]
            v_ = nc.vector

            def link_(ins):
                link(dve, dch, chain, ins)

            tt_, ts_, stt = v_.tensor_tensor, v_.tensor_scalar, v_.scalar_tensor_tensor
            done = [0]

            def split_to(v_end):
                while done[0] < v_end:
                    v = done[0]
                    slot, w = v % RING, unit_width(v)
                    dve.wait_ge(hi_done, v + 1)
                    tt_(LO[:, slot, 0:w], RAW[:, RAW_OF_W[v] % RING, 0:w], HI[:, slot, 0:w].bitcast(F32), ALU.subtract)\
                        .then_inc(lo_done, 1)
                    done[0] += 1

            def cmul(out, x, y, t):
                tt_(out[0], x[0], y[0], ALU.mult)
                tt_(t[0], x[1], y[1], ALU.mult)
                tt_(out[1], x[0], y[1], ALU.mult)
                link_(tt_(t[1], x[1], y[0], ALU.mult))
                tt_(out[0], out[0], t[0], ALU.subtract)
                ins = tt_(out[1], out[1], t[1], ALU.add)
                return ins

            def reduce_angle(r, x, k, quarter):
                link_(ts_(k, x, INV_2PI, quarter, ALU.mult, ALU.add))
                link_(ts_(k, k, ROUND, None, ALU.add))
                link_(ts_(k, k, -ROUND, None, ALU.add))
                link_(stt(out=r, in0=k, scalar=-TWO_PI_1, in1=x, op0=ALU.mult, op1=ALU.add))
                link_(stt(out=r, in0=k, scalar=-TWO_PI_2, in1=r, op0=ALU.mult, op1=ALU.add))
                link_(stt(out=r, in0=k, scalar=-TWO_PI_3, in1=r, op0=ALU.mult, op1=ALU.add))
                if quarter:
                    link_(ts_(r, r, math.pi / 2, None, ALU.add))
                return ts_(r, r, PI_SAFE, -PI_SAFE, ALU.min, ALU.max)

            def sm(i, n=1):
                return SM[:, i, :] if n == 1 else SM[:, i:i + n, :]

            dve.wait_ge(a_in, 48)
            v_.tensor_copy(AROWS[64:96, :, :], LDT[64:96, :].unsqueeze(2).broadcast_to([32, 2, NS])).then_inc(ldt_ok, 1)
            dve.wait_ge(vec_ps, 1)
            v_.tensor_copy(VEC[:, 0:85], PS[:, 2, 0:85]).then_inc(vec_ok, 1)
            dve.wait_ge(at_ps, 1)
            v_.tensor_copy(AT[:, :], PS[:, 3, 0:96]).then_inc(at_ok, 1)
            dve.wait_ge(at_ok, 1)
            are, aim = AT[:, 0:32], AT[:, 32:64]
            tt_(sm(24), are, are, ALU.mult)
            link_(tt_(sm(25), aim, aim, ALU.mult))
            link_(tt_(sm(24), sm(24), sm(25), ALU.add))
            v_.reciprocal(sm(24), sm(24))
            dve.wait_ge(dt_ok, 1)
            tt_(sm(1), are, sm(0), ALU.mult).then_inc(tre_ok, 1)
            link_(tt_(sm(2), aim, sm(0), ALU.mult))
            for i, f in enumerate((1.0, 0.5, float(L), 1.0, float(L))):
                last = ts_(sm(8 + i), sm(2), f, None, ALU.mult)
            link_(last)
            link_(reduce_angle(sm(3, 3), sm(8, 3), sm(26, 3), 0.0))
            reduce_angle(sm(6, 2), sm(11, 2), sm(26, 2), 0.25).then_inc(ang_ok, 1)
            dve.wait_ge(cact_ok, 1)
            v_.tensor_copy(CB[:, :, :], ST[:, 24:32].unsqueeze(2).broadcast_to([P, DT, 32])).then_inc(cb_ok, 1)
            dve.wait_ge(fun_ok, 2)
            ar, ai = PW[:, 0, :, 1], PW[:, 1, :, 1]
            v_.memset(PW[:, 0, :, 0], 1.0)
            v_.memset(PW[:, 1, :, 0], 0.0)
            tt_(ar, sm(18), sm(16), ALU.mult)
            tt_(ai, sm(18), sm(13), ALU.mult)
            link_(ts_(sm(25), sm(18), 1.0, None, ALU.add))
            tt_(sm(25), sm(19), sm(25), ALU.mult)
            link_(tt_(sm(26), sm(14), sm(14), ALU.mult))
            link_(tt_(sm(25), sm(25), sm(16), ALU.mult))
            link_(stt(out=sm(25), in0=sm(26), scalar=-2.0, in1=sm(25), op0=ALU.mult, op1=ALU.add))
            tt_(sm(27), sm(25), are, ALU.mult)
            tt_(sm(28), ai, aim, ALU.mult)
            tt_(sm(29), ai, are, ALU.mult)
            link_(tt_(sm(30), sm(25), aim, ALU.mult))
            tt_(sm(27), sm(27), sm(28), ALU.add)
            link_(tt_(sm(29), sm(29), sm(30), ALU.subtract))
            tt_(sm(31), sm(27), sm(24), ALU.mult)
            link_(tt_(sm(32), sm(29), sm(24), ALU.mult))
            tb = [RTMP[:, i, :].rearrange("p (g h) -> p g h", g=GI) for i in range(2)]
            dve.wait_ge(bn_in, 64)
            fb = [sm(31 + i).unsqueeze(2).broadcast_to([P, GI, GH]) for i in range(2)]
            link_(cmul([BB[:, c, :, :] for c in range(2)], fb, [BN[:, c, :, :] for c in range(2)], tb))
            def pw(t0, t1):
                return [PW[:, c, :, t0:t1] for c in range(2)]

            def tmp(n):
                return [RTMP[:, i, 0:GI * n].rearrange("p (g n) -> p g n", g=GI) for i in range(2)]

            link_(cmul(pw(2, 3), pw(1, 2), pw(1, 2), tmp(1)))
            for m in (2, 4):
                y = [a.broadcast_to([P, GI, m]) for a in pw(m, m + 1)]
                link_(cmul(pw(m + 1, 2 * m + 1), pw(1, m + 1), y, tmp(m)))
            ts_(PW[:, 2:4, :, :], PW[:, 0:2, :, :], -1.0, None, ALU.mult).then_inc(pw_ok, 1)
            for t in range(L):
                last = v_.tensor_copy(PWR[:, :, :, t], PW[:, 0:2, :, L - 1 - t])
            last.then_inc(bb_ok, 1)
            dve.wait_ge(bb_ok, 1)

            def r_block(r):
                g = slice(4 * r, 4 * r + 4)
                if r:
                    dve.wait_ge(rt_ps, 2 * r)
                sh = [P, 4, L, GH]
                p = [PWR[:, c, g, :].unsqueeze(3).broadcast_to(sh) for c in range(2)]
                b = [BB[:, c, g, :].unsqueeze(2).broadcast_to(sh) for c in range(2)]
                o = [RBLK[:, c, :, :, :] for c in range(2)]
                t = [RTMP[:, i, :].rearrange("p (g t h) -> p g t h", g=4, t=L) for i in range(2)]
                tt_(o[0], p[0], b[0], ALU.mult)
                tt_(t[0], p[1], b[1], ALU.mult)
                tt_(o[1], p[0], b[1], ALU.mult)
                link_(tt_(t[1], p[1], b[0], ALU.mult))
                tt_(o[0], o[0], t[0], ALU.subtract).then_inc(rblk_ok, 1)
                tt_(o[1], o[1], t[1], ALU.add).then_inc(rblk_ok, 1)

            def mod_rows(s):
                dve.wait_ge(row_in[s % 2], 16 * (s // 2 + 1))
                dve.wait_ge(bias_in[s % 2], 32 * (s // 2 + 1))
                rows = MROW[:, s % 2, :]
                if s in GATES:
                    link_(tt_(rows, rows, BROW[:, s % 2, :], ALU.add))
                    tt_(rows, rows, NROW[:, s % 2, :], ALU.mult).then_inc(mrow_ok, 1)
                else:
                    tt_(rows, rows, BROW[:, s % 2, :], ALU.add).then_inc(mrow_ok, 1)

            def mod_columns(s):
                bank = (4 if s < 6 else 6) + s % 2
                n = sum(1 for i in range(s + 1) if i not in GATES)
                dve.wait_ge(mod_ps, n)
                src = PS[:, bank, 256:256 + DT]
                l, kind = divmod(s, 6)
                if kind in (1, 4):
                    w = VEC[:, (4 * l + (0 if kind == 1 else 2)) * DT:(4 * l + (0 if kind == 1 else 2) + 1) * DT]
                    stt(out=MOD[:, s, :], in0=src, scalar=1.0, in1=w, op0=ALU.add, op1=ALU.mult).then_inc(mod_ok, 1)
                else:
                    v_.tensor_copy(MOD[:, s, :], src).then_inc(mod_ok, 1)

            def norm_rows(m, src, dst):
                dve.wait_ge(n_rt, m + 1)
                link_(v_.reciprocal(ST[:, 8:10], ST[:, 6:8]))
                for tt in range(TT):
                    ts_(dst[:, tt, :], src[:, tt, :], ST[:, 8 + tt:9 + tt], None, ALU.mult).then_inc(n_tok, 1)

            def columns(m, dt):
                s = 6 * (m // 2) + 3 * (m % 2)
                return MOD[:, s + 1, dt:dt + 1], MOD[:, s, dt:dt + 1]

            def norm_columns(m, split=True):
                dve.wait_ge(mod_ok, 2 * (m + 1))
                for dt in range(DT):
                    dve.wait_ge(n_ps, 4 * m + dt // 2 + 1)
                    a, b = columns(m, dt)
                    ts_(H32[:, dt, :], PS[:, 6 + (dt // 2) % 2, (dt % 2) * SEQ:(dt % 2 + 1) * SEQ], a, b, ALU.mult, ALU.add)\
                        .then_inc(n_f32, 1)
                    if split and dt >= 2:
                        norm_lo(m, dt - 2)
                if split:
                    norm_lo(m, DT - 2)
                    norm_lo(m, DT - 1)

            def norm_lo(m, dt):
                dve.wait_ge(n_hi, DT * (m - 1) + dt + 1)
                tt_(AL[:, dt, :], H32[:, dt, :], AH[:, dt, :].bitcast(F32), ALU.subtract).then_inc(n_lo, 1)

            def o_part(q):
                dve.wait_ge(ct_ok, 2)
                return o_chunk(v_, link_, [RTMP[:, i, :] for i in range(2)], q)

            norm_rows(0, XN0, XN0)
            for r in range(4):
                r_block(r)
            dve.wait_ge(rblk_ok, 8)
            link_(o_part(O_ON_POOL))
            mod_rows(0)
            mod_rows(1)
            mod_columns(0)
            mod_columns(1)
            dve.wait_ge(mod_ok, 2)
            for dt in range(DT):
                dve.wait_ge(n_ps, dt // 2 + 1)
                a, b = columns(0, dt)
                src = PS[:, 6 + (dt // 2) % 2, (dt % 2) * SEQ:(dt % 2 + 1) * SEQ].rearrange("p (j t) -> p t j", t=L)
                ts_(UT[:, dt, :, :], src, a, b, ALU.mult, ALU.add).then_inc(n_f32, 1)
            r_block(4)
            dve.wait_ge(rblk_ok, 10)
            link_(o_part(O_ON_POOL + 1))
            v_.memset(TAB[:, 0, :, 0:1], 1.0).then_inc(o_ok, 1)
            for r in range(5, 8):
                r_block(r)
            link_(v_.memset(TAB[:, 1, :, 0:1], 0.0))
            z = [sm(17), sm(15)]
            nz = [sm(33), sm(34)]
            m = 1
            while m < NJ:
                y = [a.unsqueeze(2).broadcast_to([P, GI, m]) for a in z]
                link_(cmul([TAB[:, c, :, m:2 * m] for c in range(2)], [TAB[:, c, :, 0:m] for c in range(2)], y, tmp(m)))
                if 2 * m < NJ:
                    t1, t2 = sm(27), sm(28)
                    tt_(t1, z[0], z[0], ALU.mult)
                    tt_(t2, z[1], z[1], ALU.mult)
                    link_(tt_(nz[1], z[0], z[1], ALU.mult))
                    tt_(nz[0], t1, t2, ALU.subtract)
                    link_(ts_(nz[1], nz[1], 2.0, None, ALU.mult))
                    z, nz = nz, z
                m *= 2
            dve.wait_ge(o_ok, 2)
            v_.memset(R8T[:, :, 0:1], 0.0)
            v_.tensor_copy(R8T[:, :, 1:], sm(20).unsqueeze(2).broadcast_to([P, GI, NJ - 1])).then_inc(tab_ok, 1)
            dve.wait_ge(tab_ok, 1)
            mod_rows(2)
            mod_rows(3)
            mod_columns(3)
            dve.wait_ge(v_ps, 1)
            cos, sin = TAB[:, 0, :, :], TAB[:, 1, :, :]
            vv = [PS[:, 2 * c:2 * c + 2, :].rearrange("p b (g j) -> p (b g) j", j=NJ) for c in range(2)]
            t = TMP[:, 0, :, :]
            tt_(G[:, 0, :, :], vv[0], cos, ALU.mult)
            link_(tt_(t, vv[1], sin, ALU.mult))
            tt_(G[:, 1, :, :], vv[1], cos, ALU.mult)
            link_(tt_(G[:, 0, :, :], G[:, 0, :, :], t, ALU.add))
            link_(tt_(t, vv[0], sin, ALU.mult))
            link_(tt_(G[:, 1, :, :], G[:, 1, :, :], t, ALU.subtract))
            flat = lambda a: a.rearrange("p g j -> p (g j)")
            for c in range(2):
                last = v_.tensor_tensor_scan(flat(G[:, c, :, :]), flat(R8T[:, :, :]), flat(G[:, c, :, :]), 0.0, ALU.mult, ALU.add)
            link_(last)
            dve.wait_ge(m_in, 16 * 32)
            v_.memset(S[:, :, :, 0:1], 0.0)
            g0, g1 = [G[:, c, :, 0:NJ - 1] for c in range(2)]
            cos, sin, t = cos[:, :, 0:NJ - 1], sin[:, :, 0:NJ - 1], t[:, :, 0:NJ - 1]
            tt_(S[:, 0, :, 1:], g0, cos, ALU.mult)
            link_(tt_(t, g1, sin, ALU.mult))
            tt_(S[:, 1, :, 1:], g1, cos, ALU.mult)
            link_(tt_(S[:, 0, :, 1:], S[:, 0, :, 1:], t, ALU.subtract))
            link_(tt_(t, g0, sin, ALU.mult))
            tt_(S[:, 1, :, 1:], S[:, 1, :, 1:], t, ALU.add).then_inc(s_ok, 1)
            mod_rows(4)
            mod_columns(4)
            mod_rows(5)
            split_to(2)
            dve.wait_ge(yt_in, 16)
            for dt in range(DT):
                stt(out=YT[:, dt, :, :], in0=UT[:, dt, :, :], scalar=VEC[:, 64 + dt:65 + dt], in1=YT[:, dt, :, :],
                    op0=ALU.mult, op1=ALU.add).then_inc(yt_ok, 1)
            for dt in range(DT):
                dve.wait_ge(zh_ok, dt + 1)
                tt_(AL[:, dt, :], H32[:, dt, :], AH[:, dt, :].bitcast(F32), ALU.subtract).then_inc(zl_ok, 1)
            split_to(6)
            for n in range(4):
                for tt in range(TT):
                    dve.wait_ge(sig_ok, 2 * n + tt + 1)
                    tt_(TOK[:, tt, n * FB:(n + 1) * FB], PS[:, 2 * (n % 2) + tt, 0:FB], SG[:, n % 2, tt, :], ALU.mult)\
                        .then_inc(glu_ok, 1)
                split_to(min(8 + 2 * n, V_FFN + 4))
            split_to(V_FFN + 4)

            def residual(n, pieces):
                dve.wait_ge(r_ss, n + 1)
                tt_(ST[:, 14:16], ST[:, 10:14:2], ST[:, 11:14:2], ALU.add).then_inc(r_sum, 1)
                dve.wait_ge(r_rt, n + 1)
                link_(v_.reciprocal(ST[:, 18:20], ST[:, 16:18]))
                dve.wait_ge(gate_in, 16 * (n + 1))
                for i, src in enumerate(pieces):
                    last = stt(out=RES[:, i, :], in0=src, scalar=ST[:, 18 + i // 2:19 + i // 2],
                               in1=GROW[:, (i % 2) * 512:(i % 2 + 1) * 512], op0=ALU.mult, op1=ALU.mult)
                link_(last)
                for i in range(4):
                    x = X[:, i // 2, (i % 2) * 512:(i % 2 + 1) * 512]
                    last = tt_(x, x, RES[:, i, :], ALU.add)
                    if i % 2:
                        last.then_inc(res_ok, 1)

            dve.wait_ge(x_ld, 32)
            residual(0, [TOK[:, i // 2, (i % 2) * 512:(i % 2 + 1) * 512] for i in range(4)])
            norm_rows(1, X, TOK)
            norm_columns(1)
            for t in range(FSTEPS):
                va = V_FFN + 3 * t - (1 if t else 0)
                for ft in range(2):
                    f = 2 * t + ft
                    split_to(va + 4 + ft if t else V_FFN + 3 + ft)
                    dve.wait_ge(f_silu, f + 1)
                    if f >= 4:
                        dve.wait_ge(f_hi, f - 3)
                    tt_(FP[:, f % 4, :], FS[:, f % 4, :], PS[:, 4 + f % 2, SEQ:2 * SEQ], ALU.mult).then_inc(f_prod, 1)
                    if ft == 0 and t:
                        split_to(va + 5)
                    dve.wait_ge(f_hi, f + 1)
                    tt_(GTL[:, f % 4, :], FP[:, f % 4, :], GTH[:, f % 4, :].bitcast(F32), ALU.subtract).then_inc(f_lo, 1)
                    if ft == 1 and t % 2:
                        mod_rows(6 + t // 2)
                    if ft == 1 and t and t % 2 == 0 and 5 + t // 2 not in GATES:
                        mod_columns(5 + t // 2)
                split_to(va + 6 if t else V_FFN + 5)
            mod_rows(NSEC - 1)
            dve.wait_ge(unit_used, V_MLA)
            residual(1, [PS[:, i, :] for i in range(4)])
            norm_rows(2, X, TOK)
            norm_columns(2)
            split_to(V_MLA + 6)
            dve.wait_ge(pos_ld, 16)
            dve.wait_ge(iota_ok, 1)
            link_(v_.tensor_copy(POSF[:, :], POSI[:, :]))
            for tt in range(TT):
                last = ts_(ROT[:, 0, tt, :], INVF[:, :], POSF[:, tt:tt + 1], None, ALU.mult)
            link_(last)
            link_(reduce_angle(ROT[:, 2, :, :], ROT[:, 0, :, :], ROT[:, 1, :, :], 0.0))
            reduce_angle(ROT[:, 3, :, :], ROT[:, 0, :, :], ROT[:, 1, :, :], 0.25).then_inc(cs_arg, 1)
            dve.wait_ge(p_rt, 1)
            link_(v_.reciprocal(ST[:, 8:12], ST[:, 4:8]))
            for tt in range(TT):
                q, kv = PR[:, tt, 0:QR], PR[:, tt, QR:QR + KR]
                ts_(q, q, ST[:, 8 + tt:9 + tt], None, ALU.mult)
                ts_(kv, kv, ST[:, 10 + tt:11 + tt], None, ALU.mult).then_inc(p_nrm, 1)
            for i in range(5):
                dve.wait_ge(p_ps, min(i - i % 2 + 2, 5))
                ts_(C32[:, i, :], PS[:, (6, 7, 5)[i // 2], (i % 2) * SEQ:(i % 2 + 1) * SEQ], VEC[:, 80 + i:81 + i], None,
                    ALU.mult).then_inc(p_f32, 1)
            for i in range(5):
                dve.wait_ge(p_hi, i + 1)
                tt_(CQL[:, i, :], C32[:, i, :], CQH[:, i, :].bitcast(F32), ALU.subtract).then_inc(p_lo, 1)
            dve.wait_ge(p_lo, 5)
            dve.wait_ge(cs_ok, 1)
            dve.wait_ge(gate_out[3], 16)

            def rotate(dst, src, tt, n):
                sh = [P, n, HALF]
                cos, sin = [CS[:, i, tt, :].unsqueeze(1).broadcast_to(sh) for i in range(2)]
                x1, x2 = src[:, :, 0:HALF], src[:, :, HALF:]
                r = [RTM[:, i, 0:n, :] for i in range(4)]
                tt_(r[0], x1, cos, ALU.mult)
                tt_(r[1], x2, sin, ALU.mult)
                tt_(r[2], x1, sin, ALU.mult)
                link_(tt_(r[3], x2, cos, ALU.mult))
                tt_(dst[:, :, 0:HALF], r[0], r[1], ALU.subtract)
                return tt_(dst[:, :, HALF:], r[2], r[3], ALU.add)

            for tt in range(TT):
                kr = PR[:, tt, QR + KR:].unsqueeze(1)
                link_(rotate(kr, kr, tt, 1))
                v_.tensor_copy(KF[:, tt, :, NOPE:], kr.broadcast_to([P, H, ROPE])).then_inc(k_rope, 2)
            dve.wait_ge(k_rope, 4)
            split_to(V_MLA + 8)
            for tt in range(TT):
                if tt:
                    dve.wait_ge(q_rope, tt)
                dve.wait_ge(q_sb, 3 * (tt + 1))
                qr = Q[:, tt, :, NOPE:]
                rotate(qr, qr, tt, H).then_inc(q_rope, 1)
            split_to(V_MLA + 9)
            dve.wait_ge(unit_used, V_MLA + 8)
            for b in range(4):
                kv = PS[:, 2 + b, :].rearrange("p (h d) -> p h d", h=4)
                v_.tensor_copy(KF[:, 1, 4 * b:4 * b + 4, 0:NOPE], kv[:, :, 0:NOPE]).then_inc(kf_ok, 1)
                v_.tensor_copy(VV[:, 1, 4 * b:4 * b + 4, :], kv[:, :, NOPE:]).then_inc(vv_ok, 1)
            split_to(V_MLA + 12)
            dve.wait_ge(mask_ok, 1)
            dve.wait_ge(q_rope, 2)
            for i in range(H + 3):
                h = i - 2
                if 0 <= h < H:
                    b = h % 2
                    dve.wait_ge(e_ok, h + 1)
                    link_(v_.reciprocal(ST[:, 16 + 2 * b:18 + 2 * b], ST[:, 8 + 2 * b:10 + 2 * b]))
                    ts_(PB[:, b, 0:P], PB[:, b, 0:P], ST[:, 16 + 2 * b:17 + 2 * b], None, ALU.mult)
                    ts_(PB[:, b, P:], PB[:, b, P:], ST[:, 17 + 2 * b:18 + 2 * b], None, ALU.mult).then_inc(pn_ok, 1)
                h = i - 1
                if 0 <= h < H:
                    b = h % 2
                    dve.wait_ge(s_mm, h + 1)
                    if h >= 2:
                        dve.wait_ge(pt_ps, h - 1)
                    for tt in range(TT):
                        c0, c1 = (0, P) if tt == 0 else (P, 3 * P)
                        last = v_.tensor_tensor_reduce(
                            out=PB[:, b, c0:c1], in0=PS[:, 2 + b, c0:c1], in1=MASK[:, P if tt == 0 else 0:],
                            scale=1.0, scalar=3 * NEG, op0=ALU.add, op1=ALU.max, accum_out=ST[:, 12 + 2 * b + tt:13 + 2 * b + tt])
                    link_(last)
                    ts_(ST[:, 4 + 2 * b:6 + 2 * b], ST[:, 12 + 2 * b:14 + 2 * b], -SCALE, None, ALU.mult).then_inc(s_max, 1)
                h = i - 3
                if h >= 0 and h % 2:
                    dve.wait_ge(o_hi, h // 2 + 1)
                    tt_(OTL[:, h // 2, :], PS[:, 6 + (h // 2) % 2, 0:SEQ], OTH[:, h // 2, :].bitcast(F32), ALU.subtract)\
                        .then_inc(o_lo, 1)
            def one_hot(e, b, first=False):
                if not first:
                    dve.wait_ge(pt1_ps, e - 1)
                for tt in range(TT):
                    v_.tensor_copy(HOT[:, b, 0, tt:tt + 1], SLOT[:, tt, bass.ds(e, 1)])
                    last = v_.tensor_copy(HOT[:, b, 1, tt:tt + 1], COMBP[:, tt, bass.ds(e, 1)])
                last.then_inc(hot_ok, 1)
                dve.wait_ge(hot_ok, e * 2 + 1)
                for tt in range(TT):
                    last = ts_(ONE[:, b, tt, :], IOTA[:, :], HOT[:, b, 0, tt:tt + 1], None, ALU.is_equal)
                last.then_inc(hot_ok, 1)

            split_to(V_MOE + 2)
            dve.wait_ge(unit_used, V_MOE)
            dve.wait_ge(x_ld, 48)
            residual(2, [PS[:, i, :] for i in range(4)])
            norm_rows(3, X, TOK)
            norm_columns(3, split=False)
            dve.wait_ge(lg_ps, 1)
            dve.wait_ge(rc_in, 32)
            tt_(LG[:, :, :], PS[:, 5, 0:TT * NE].rearrange("p (t e) -> p t e", t=TT),
                BRT[:, :].unsqueeze(1).broadcast_to([P, TT, NE]), ALU.add)
            link_(v_.memset(WT[:, 3, :], 0.0))
            for tt in range(TT):
                last = v_.max(M8[:, tt, :], LG[:, tt, :])
            link_(last)
            for tt in range(TT):
                last = v_.max_index(I8[:, tt, :], M8[:, tt, :], LG[:, tt, :])
            link_(last)
            v_.tensor_copy(IF[:, :, :], I8[:, :, 0:2])
            tt_(WT[:, 0, :], M8[:, :, 1], M8[:, :, 0], ALU.subtract).then_inc(td_ok, 1)
            dve.wait_ge(te_ok, 1)
            link_(ts_(WT[:, 2, :], WT[:, 1, :], 1.0, None, ALU.add))
            link_(v_.reciprocal(WT[:, 2, :], WT[:, 2, :]))
            link_(tt_(WT[:, 3, :], WT[:, 1, :], WT[:, 2, :], ALU.mult))
            for tt in range(TT):
                for i in range(2):
                    last = ts_(SEL[:, i, tt, :], IOTA[:, 0:NE], IF[:, tt, i:i + 1], None, ALU.is_equal)
            link_(last)
            tt_(MSK[:, :, :], SEL[:, 0, :, :], SEL[:, 1, :, :], ALU.add).then_inc(msk_ok, 1)
            for tt in range(TT):
                last = ts_(COMB[:, tt, :], SEL[:, 0, tt, :], WT[:, 2, tt:tt + 1], None, ALU.mult)
            link_(last)
            for tt in range(TT):
                last = stt(out=COMBP[:, tt, :], in0=SEL[:, 1, tt, :], scalar=WT[:, 3, tt:tt + 1], in1=COMB[:, tt, :],
                           op0=ALU.mult, op1=ALU.add)
            link_(last)
            link_(ts_(SEL[:, 0, :, :], MSK[:, :, :], -1e4, 1e4, ALU.mult, ALU.add))
            dve.wait_ge(pos_ps, 1)
            link_(tt_(SLOT[:, :, :], SEL[:, 0, :, :], PS[:, 4, 0:TT * NE].rearrange("p (t e) -> p t e", t=TT), ALU.add))
            one_hot(0, 0, first=True)
            def gather_lo(e, b, r):
                dve.wait_ge(g_hi, e * 2 + r + 1)
                q = slice(4 * r, 4 * r + 4)
                tt_(XEL[:, b, q, :], XE32[:, q, :], XEH[:, b, q, :].bitcast(F32), ALU.subtract).then_inc(g_lo, 1)

            def add_piece(e, i, first, bank=7):
                tt, dh = divmod(i, 2)
                dst = YACC[:, tt, dh * 512:(dh + 1) * 512]
                dve.wait_ge(sc_mm, e * 4 + i + 1)
                if first:
                    v_.tensor_copy(dst, PS[:, bank, :]).then_inc(acc_ok, 1)
                else:
                    tt_(dst, dst, PS[:, bank, :], ALU.add).then_inc(acc_ok, 1)

            def split_moe(i, m):
                slot = (V_MOE + m) % RING
                dve.wait_ge(hi_done, moe_at(i, m) + 1)
                tt_(LO[:, slot, :], RAW[:, (RAW_OF_W[V_MOE] + m) % RING, :], HI[:, slot, :].bitcast(F32), ALU.subtract)\
                    .then_inc(lo_done, 1)

            def products_lo(i, tau):
                dve.wait_ge(t_hi, i * (2 * MSTEPS) + tau + 1)
                tt_(EGL[:, tau % 2, :, :].rearrange("p a s -> p (a s)"), PS[:, 6, 0:2 * P],
                    EGH[:, tau % 2, :, :].rearrange("p a s -> p (a s)").bitcast(F32), ALU.subtract).then_inc(t_lo, 1)

            def expert_pair(i, first, last_pair):
                for tau in range(2 * MSTEPS):
                    j, s = divmod(tau, MSTEPS)
                    e = i * 2 + j
                    start, end = first and j == 0, last_pair and j == 1
                    up_next = not (last_pair and tau == 2 * MSTEPS - 1)
                    na, nb, _ = moe_units(first, last_pair, tau + 1)
                    if up_next:
                        split_moe(i, na)
                    if s == 1 and not end:
                        one_hot(e + 1, 1 - j, first=start)
                    if s == 6 and not end:
                        gather_lo(e + 1, 1 - j, 0)
                    if not (first and tau == 0):
                        products_lo(i, tau - 1)
                    if up_next:
                        split_moe(i, nb)
                    split_moe(i, moe_units(first, last_pair, tau)[2])
                    t = i * (2 * MSTEPS) + tau
                    dve.wait_ge(e_silu, t + 1)
                    if not (first and tau < 2):
                        dve.wait_ge(t_ps, t - 1)
                    tt_(EPR[:, tau % 2, :], ESI[:, tau % 2, :], PS[:, 4 + tau % 2, FB:], ALU.mult).then_inc(e_prod, 1)
                    if 1 <= s <= 4 and not start:
                        add_piece(e - 1, s - 1, first and j == 1)
                    if s == 6 and not end:
                        gather_lo(e + 1, 1 - j, 1)

            v_.tensor_copy(CNT[:, 0:NE], PS[:, 4, 2 * NE:3 * NE])
            link_(v_.tensor_reduce(ST[:, 20:21], PS[:, 4, 2 * NE:3 * NE], AX.X, ALU.max))
            v_.tensor_copy(CNT[:, NE:NE + 1], ST[:, 20:21]).then_inc(ovf_ok, 1)
            most = most_crowded(dve)

            for r in range(2):
                gather_lo(0, 0, r)
            moe_loop(dve, expert_pair)
            products_lo(NE // 2 - 1, 2 * MSTEPS - 1)
            for i in range(4):
                add_piece(NE - 1, i, False, bank=4 + i % 3)

            def second_pass(e, k):
                for tt in range(TT):
                    ts_(VC[:, 0, tt:tt + 1], SLOT[:, tt, bass.ds(e, 1)], -float(P), None, ALU.add)
                    last = v_.tensor_copy(VC[:, 1, tt:tt + 1], COMBP[:, tt, bass.ds(e, 1)])
                last.then_inc(v_hot, 1)
                dve.wait_ge(v_hot, k * 3 + 1)
                for tt in range(TT):
                    last = ts_(VH[:, 0, tt, :], IOTA[:, :], VC[:, 0, tt:tt + 1], None, ALU.is_equal)
                last.then_inc(v_hot, 1)
                dve.wait_ge(v_hot, k * 3 + 2)
                for tt in range(TT):
                    last = ts_(VH[:, 1, tt, :], VH[:, 0, tt, :], VC[:, 1, tt:tt + 1], None, ALU.mult)
                last.then_inc(v_hot, 1)
                dve.wait_ge(v_gps, k + 1)
                v_.tensor_copy(PT[:, :], PS[:, 5, 0:SEQ])
                for dt in range(DT):
                    a, b = columns(3, dt)
                    last = ts_(VX[:, dt, :], PS[:, 6 + dt // 4, (dt % 4) * P:(dt % 4 + 1) * P], a, b, ALU.mult, ALU.add)
                last.then_inc(v_x, 1)
                for s in range(MSTEPS):
                    dve.wait_ge(v_silu, k * MSTEPS + s + 1)
                    tt_(EPR[:, s % 2, :], ESI[:, s % 2, :], PS[:, 4 + s % 2, FB:], ALU.mult).then_inc(v_prod, 1)
                    dve.wait_ge(v_tps, k * MSTEPS + s + 1)
                    v_.tensor_copy(VT[:, s % 2, :, :].rearrange("p a s -> p (a s)"), PS[:, 6 + s % 2, 0:2 * P])\
                        .then_inc(v_t, 1)
                dve.wait_ge(v_sc, k + 1)
                for i in range(4):
                    dst = YACC[:, i // 2, (i % 2) * 512:(i % 2 + 1) * 512]
                    last = tt_(dst, dst, PS[:, 2 + i, :], ALU.add)
                last.then_inc(v_acc, 1)
                dve.wait_ge(v_acc, k + 1)

            second_passes(dve, most, second_pass)
            residual(3, [YACC[:, i // 2, (i % 2) * 512:(i % 2 + 1) * 512] for i in range(4)])


_NAMES = ["x", "c", "positions", "norm_g", "w_ada", "b_ada", "ssm_a_re", "ssm_a_im", "ssm_log_dt", "ssm_b_re",
          "ssm_b_im", "ssm_c_re", "ssm_c_im", "ssm_d", "ssm_w_glu", "ffn_w_in", "ffn_w_out", "mla_w_in", "mla_q_norm",
          "mla_kv_norm", "mla_w_uq", "mla_w_ukv", "mla_w_o", "moe_w_router", "moe_b_router", "moe_w_in", "moe_w_out"]
_KEEP = ("x", "c", "positions", "norm_g", "w_ada", "b_ada")


def kernel(**inputs):
    import concourse.bacc as bacc
    from concourse.bass_utils import run_bass_kernel_spmd

    nc = bacc.Bacc("TRN2", target_bir_lowering=False, num_devices=1)
    arrays, args = {}, []
    for name in _NAMES:
        a = np.ascontiguousarray(inputs[name])
        if name not in _KEEP:
            a = a[0]
        arrays[f"in_{name}"] = a
        args.append(nc.dram_tensor(f"in_{name}", a.shape, mybir.dt.from_np(a.dtype), kind="ExternalInput").ap())
    args.append(nc.dram_tensor("out_0", (1, SEQ, D), F32, kind="ExternalOutput").ap())
    program(nc, *args)
    r = run_bass_kernel_spmd(nc, [arrays], core_ids=[0])
    return r.results[0]["out_0"]
```
